# Optimizing a Trainium2 kernel written in Bass

```python
import jax
import jax.numpy as jnp
from jax import lax
import numpy as np
import jax, jax.numpy as jnp

D_MODEL = 1024
BATCH = 1
SEQ = 512
DEPTH = 1

GRID_W = 64
CTX_LEN = 256
D_MIX = D_MODEL
GLA_WIDTH = D_MIX // 2
GLA_HEADS = 4
GLA_DV = GLA_WIDTH // GLA_HEADS
GLA_DK = GLA_DV // 2
GLA_QK = GLA_HEADS * GLA_DK
GLA_LOWRANK = 16
GLA_TAU = 16.0
GLA_CHUNK = 64
SC_WIDTH = D_MIX - GLA_WIDTH
D_FF = 2816
EPS = 1e-6

COL_K = 0
COL_V = COL_K + GLA_QK
COL_AF = COL_V + GLA_WIDTH
COL_AB = COL_AF + GLA_LOWRANK
COL_Q = COL_AB + GLA_LOWRANK
COL_OG = COL_Q + GLA_QK
COL_SB = COL_OG + GLA_WIDTH
COL_SC = COL_SB + SC_WIDTH
COL_SX = COL_SC + SC_WIDTH
D_IN = COL_SX + SC_WIDTH


def rmsnorm(x, g):
    xf = x.astype(jnp.float32)
    y = xf * lax.rsqrt(jnp.mean(xf * xf, axis=-1, keepdims=True) + EPS)
    return (y * g.astype(jnp.float32)).astype(x.dtype)

def adaln(cond, w, b):
    return jax.nn.silu(cond) @ w + b

def modulate(h, shift, scale):
    return h * (1.0 + scale) + shift

def flip(a):
    return a[:, ::-1]

def gate_logdecay(a_low, w, b):
    a = (a_low @ w + b).astype(jnp.float32)
    return (jax.nn.log_sigmoid(a) / GLA_TAU).reshape(a.shape[0], a.shape[1], GLA_HEADS, GLA_DK)

def gla_inputs(p, w_af, b_af, w_ab, b_ab):
    bsz, t, _ = p.shape
    k = p[..., COL_K:COL_V].reshape(bsz, t, GLA_HEADS, GLA_DK)
    v = p[..., COL_V:COL_AF].reshape(bsz, t, GLA_HEADS, GLA_DV)
    g_f = gate_logdecay(p[..., COL_AF:COL_AB], w_af, b_af)
    g_b = gate_logdecay(p[..., COL_AB:COL_Q], w_ab, b_ab)
    return k, v, g_f, g_b

def gla_final_state(k, v, g):
    b = jnp.cumsum(g.astype(jnp.float32), axis=1)
    w = jnp.exp(b[:, -1:] - b)
    return jnp.einsum('bthk,bthv->bhkv', k.astype(jnp.float32) * w, v.astype(jnp.float32))

def gla_chunked(q, k, v, g, s0, strict):
    bsz, t, h, dk = q.shape
    dv = v.shape[-1]
    n = t // GLA_CHUNK

    def chunks(a):
        a = a.astype(jnp.float32).reshape(bsz, n, GLA_CHUNK, h, a.shape[-1])
        return jnp.moveaxis(a, 1, 0)

    pos = jnp.arange(GLA_CHUNK)
    mask = (pos[None, :] < pos[:, None]) if strict else (pos[None, :] <= pos[:, None])
    mask = mask[None, :, :, None, None]

    def step(s, inp):
        qc, kc, vc, gc = inp
        b = jnp.cumsum(gc, axis=1)
        o_inter = jnp.einsum('bihk,bhkv->bihv', qc * jnp.exp(b), s)
        decay = jnp.exp(jnp.where(mask, b[:, :, None] - b[:, None, :], -jnp.inf))
        att = jnp.einsum('bihk,bjhk,bijhk->bijh', qc, kc, decay)
        o_intra = jnp.einsum('bijh,bjhv->bihv', att, vc)
        b_last = b[:, -1]
        s_new = s * jnp.exp(b_last)[..., None] + jnp.einsum('bjhk,bjhv->bhkv', kc * jnp.exp(b_last[:, None] - b), vc)
        return s_new, o_inter + o_intra

    _, o = lax.scan(step, s0.astype(jnp.float32), (chunks(q), chunks(k), chunks(v), chunks(g)))
    return jnp.moveaxis(o, 0, 1).reshape(bsz, t, h, dv).astype(v.dtype)

def dwconv_row(u, w, b, rows, width):
    bsz, t, ch = u.shape
    up = jnp.pad(u.reshape(bsz, rows, width, ch), ((0, 0), (0, 0), (1, 1), (0, 0)))
    y = w[0] * up[:, :, :-2] + w[1] * up[:, :, 1:-1] + w[2] * up[:, :, 2:] + b
    return y.reshape(bsz, t, ch)

def dwconv_grid(u, w, b, rows, width):
    bsz, t, ch = u.shape
    up = jnp.pad(u.reshape(bsz, rows, width, ch), ((0, 0), (1, 1), (1, 1), (0, 0)))
    y = b
    for dr in range(3):
        for dc in range(3):
            y = y + w[dr, dc] * up[:, dr:dr + rows, dc:dc + width]
    return y.reshape(bsz, t, ch)

def token_mixers(p, s_f, s_b, rows, width, w_af, b_af, w_ab, b_ab, g_head, w_sc, b_sc):
    bsz, t, _ = p.shape
    k, v, g_f, g_b = gla_inputs(p, w_af, b_af, w_ab, b_ab)
    q = p[..., COL_Q:COL_OG].reshape(bsz, t, GLA_HEADS, GLA_DK) * (GLA_DK ** -0.5)
    og = p[..., COL_OG:COL_SB]
    o_f = gla_chunked(q, k, v, g_f, s_f, False)
    o_b = flip(gla_chunked(flip(q), flip(k), flip(v), flip(g_b), s_b, True))
    o_gla = rmsnorm(o_f + o_b, g_head).reshape(bsz, t, GLA_WIDTH) * jax.nn.silu(og)
    sb = p[..., COL_SB:COL_SC]
    sc = p[..., COL_SC:COL_SX]
    sx = p[..., COL_SX:D_IN]
    o_sc = sb * dwconv_row(sc * sx, w_sc, b_sc, rows, width)
    return jnp.concatenate([o_gla, o_sc], axis=-1)

def conv_ffn(h, rows, width, w_up, w_cf, b_cf, w_down):
    u, gate = jnp.split(h @ w_up, 2, axis=-1)
    u = dwconv_grid(u, w_cf, b_cf, rows, width)
    return (jax.nn.silu(u) * gate) @ w_down

def first_inputs(seed: int = 0) -> dict:
    key = jax.random.key(seed)
    ks = jax.random.split(key, 24)

    def nrm(k, shape, s):
        return jax.random.normal(k, shape, jnp.float32) * s

    L = DEPTH
    return {
        'x': nrm(ks[0], (BATCH, SEQ, D_MODEL), 1.0),
        'c': nrm(ks[1], (BATCH, D_MODEL), 1.0),
        'ctx': nrm(ks[2], (BATCH, CTX_LEN, D_MODEL), 1.0),
        'c_ctx': nrm(ks[3], (D_MODEL,), 1.0),
        'w_ada': nrm(ks[4], (L, D_MODEL, 6 * D_MODEL), D_MODEL ** -0.5),
        'b_ada': nrm(ks[5], (L, 6 * D_MODEL), 0.01),
        'g_pre_mix': 1.0 + nrm(ks[6], (L, D_MODEL), 0.05),
        'g_post_mix': 1.0 + nrm(ks[7], (L, D_MODEL), 0.05),
        'g_pre_ffn': 1.0 + nrm(ks[8], (L, D_MODEL), 0.05),
        'g_post_ffn': 1.0 + nrm(ks[9], (L, D_MODEL), 0.05),
        'w_in': nrm(ks[10], (L, D_MODEL, D_IN), D_MODEL ** -0.5),
        'w_af': nrm(ks[11], (L, GLA_LOWRANK, GLA_QK), GLA_LOWRANK ** -0.5),
        'b_af': nrm(ks[12], (L, GLA_QK), 0.1),
        'w_ab': nrm(ks[13], (L, GLA_LOWRANK, GLA_QK), GLA_LOWRANK ** -0.5),
        'b_ab': nrm(ks[14], (L, GLA_QK), 0.1),
        'g_head': 1.0 + nrm(ks[15], (L, GLA_DV), 0.05),
        'w_sc': nrm(ks[16], (L, 3, SC_WIDTH), 0.5),
        'b_sc': nrm(ks[17], (L, SC_WIDTH), 0.01),
        'w_out': nrm(ks[18], (L, D_MIX, D_MODEL), D_MIX ** -0.5),
        'w_up': nrm(ks[19], (L, D_MODEL, 2 * D_FF), D_MODEL ** -0.5),
        'w_cf': nrm(ks[20], (L, 3, 3, D_FF), 1.0 / 3.0),
        'b_cf': nrm(ks[21], (L, D_FF), 0.01),
        'w_down': nrm(ks[22], (L, D_FF, D_MODEL), D_FF ** -0.5),
    }

def first_block(x, c, ctx, c_ctx, w_ada, b_ada, g_pre_mix, g_post_mix, g_pre_ffn, g_post_ffn,
              w_in, w_af, b_af, w_ab, b_ab, g_head, w_sc, b_sc, w_out, w_up, w_cf, b_cf, w_down):
    rows = x.shape[1] // GRID_W
    ctx_len = ctx.shape[1]
    for i in range(DEPTH):
        update_ctx = i + 1 < DEPTH
        sh1, sc1, gt1, sh2, sc2, gt2 = jnp.split(adaln(c, w_ada[i], b_ada[i])[:, None, :], 6, axis=-1)
        csh1, csc1, cgt1, csh2, csc2, cgt2 = jnp.split(adaln(c_ctx, w_ada[i], b_ada[i]), 6, axis=-1)
        gla_p = (w_af[i], b_af[i], w_ab[i], b_ab[i])

        hc = modulate(rmsnorm(ctx, g_pre_mix[i]), csh1, csc1)
        pc = hc @ (w_in[i] if update_ctx else w_in[i][:, :COL_Q])
        kc, vc, gfc, gbc = gla_inputs(pc, *gla_p)
        s_f = gla_final_state(kc, vc, gfc)
        s_b = gla_final_state(flip(kc), flip(vc), flip(gbc))

        hx = modulate(rmsnorm(x, g_pre_mix[i]), sh1, sc1)
        yx = token_mixers(hx @ w_in[i], s_f, s_b, rows, GRID_W, *gla_p, g_head[i], w_sc[i], b_sc[i])
        x = x + gt1 * rmsnorm(yx @ w_out[i], g_post_mix[i])

        hx = modulate(rmsnorm(x, g_pre_ffn[i]), sh2, sc2)
        x = x + gt2 * rmsnorm(conv_ffn(hx, rows, GRID_W, w_up[i], w_cf[i], b_cf[i], w_down[i]), g_post_ffn[i])

        if update_ctx:
            zero_state = jnp.zeros_like(s_f)
            yc = token_mixers(pc, zero_state, zero_state, 1, ctx_len, *gla_p, g_head[i], w_sc[i], b_sc[i])
            ctx = ctx + cgt1 * rmsnorm(yc @ w_out[i], g_post_mix[i])
            hc = modulate(rmsnorm(ctx, g_pre_ffn[i]), csh2, csc2)
            ctx = ctx + cgt2 * rmsnorm(conv_ffn(hc, 1, ctx_len, w_up[i], w_cf[i], b_cf[i], w_down[i]), g_post_ffn[i])
    return x


POOL_WINDOWS = (2, 4, 8, 16)
N_POOL_GROUPS = len(POOL_WINDOWS)
POOL_WIDTH = D_MODEL
POOL_GROUP = POOL_WIDTH // N_POOL_GROUPS
HEAD_DIM = 64
N_Q_HEADS = D_MODEL // HEAD_DIM
N_KV_HEADS = 2
GQA_GROUP = N_Q_HEADS // N_KV_HEADS
WINDOW = 128
BLOCK = 128
ROPE_DIM = HEAD_DIM // 4
ROPE_THETA = 500000.0
Q_WIDTH = N_Q_HEADS * HEAD_DIM
KV_WIDTH = N_KV_HEADS * HEAD_DIM
CONV_WIDTH = 3
IN_WIDTH = POOL_WIDTH + Q_WIDTH + 2 * KV_WIDTH + 2 * D_MODEL


def rmsnorm_2(x, g):
    xf = x.astype(jnp.float32)
    r = lax.rsqrt(jnp.mean(xf * xf, axis=-1, keepdims=True) + EPS)
    return (xf * r * g.astype(jnp.float32)).astype(x.dtype)

def partial_rope(x, positions):
    half = ROPE_DIM // 2
    inv_freq = ROPE_THETA ** (-jnp.arange(0, ROPE_DIM, 2, dtype=jnp.float32) / ROPE_DIM)
    ang = positions.astype(jnp.float32)[..., None] * inv_freq
    cos = jnp.cos(ang)[:, :, None, :]
    sin = jnp.sin(ang)[:, :, None, :]
    xf = x.astype(jnp.float32)
    x1, x2, xp = xf[..., :half], xf[..., half:ROPE_DIM], xf[..., ROPE_DIM:]
    out = jnp.concatenate([x1 * cos - x2 * sin, x2 * cos + x1 * sin, xp], axis=-1)
    return out.astype(x.dtype)

def pool_mixer(u, w_pool, pool_scale):
    B, S, _ = u.shape
    ug = u.reshape(B, S, N_POOL_GROUPS, POOL_GROUP).astype(jnp.float32)
    cs = jnp.cumsum(ug, axis=1)
    t = jnp.arange(S, dtype=jnp.float32)
    pooled = []
    for g, w in enumerate(POOL_WINDOWS):
        csg = cs[:, :, g]
        shifted = jnp.pad(csg, ((0, 0), (w, 0), (0, 0)))[:, :S]
        count = jnp.minimum(t + 1.0, float(w))[None, :, None]
        pooled.append((csg - shifted) / count)
    pooled = jnp.stack(pooled, axis=2) - ug
    mixed = jnp.einsum('bsgc,gcd->bsgd', pooled.astype(u.dtype), w_pool)
    return mixed.reshape(B, S, POOL_WIDTH) * pool_scale

def swa_sink_attention(q, k, v, sinks):
    B, S = q.shape[0], q.shape[1]
    nb = S // BLOCK
    qb = q.reshape(B, nb, BLOCK, N_KV_HEADS, GQA_GROUP, HEAD_DIM)

    def band(t):
        tb = t.reshape(B, nb, BLOCK, N_KV_HEADS, HEAD_DIM)
        prev = jnp.pad(tb, ((0, 0), (1, 0), (0, 0), (0, 0), (0, 0)))[:, :-1]
        return jnp.concatenate([prev, tb], axis=2)

    kb, vb = band(k), band(v)
    s = jnp.einsum('bnqhgd,bnkhd->bhgnqk', qb, kb,
                   preferred_element_type=jnp.float32)
    q_pos = jnp.arange(BLOCK)[:, None] + BLOCK
    k_pos = jnp.arange(2 * BLOCK)[None, :]
    rel_ok = (k_pos <= q_pos) & (q_pos - k_pos < WINDOW)
    blk_ok = (jnp.arange(nb)[:, None, None] > 0) | (k_pos[None] >= BLOCK)
    mask = rel_ok[None] & blk_ok
    s = jnp.where(mask, s, -jnp.inf)
    sink = sinks.astype(jnp.float32).reshape(1, N_KV_HEADS, GQA_GROUP, 1, 1, 1)
    m = jnp.maximum(jnp.max(s, axis=-1, keepdims=True), sink)
    p = jnp.exp(s - m)
    denom = jnp.sum(p, axis=-1, keepdims=True) + jnp.exp(sink - m)
    probs = (p / denom).astype(v.dtype)
    out = jnp.einsum('bhgnqk,bnkhd->bnqhgd', probs, vb)
    return out.reshape(B, S, Q_WIDTH)

def causal_depthwise_conv(u, w, b):
    S = u.shape[1]
    up = jnp.pad(u, ((0, 0), (CONV_WIDTH - 1, 0), (0, 0)))
    y = b
    for j in range(CONV_WIDTH):
        y = y + w[j] * up[:, j:j + S]
    return y

def second_inputs(seed: int = 0) -> dict:
    key = jax.random.key(seed)
    ks = jax.random.split(key, 18)
    f32 = jnp.float32
    nrm = lambda k, shape, s: jax.random.normal(k, shape, f32) * s
    x = jax.random.normal(ks[0], (BATCH, SEQ, D_MODEL), f32)
    offsets = jax.random.randint(ks[1], (BATCH, 1), 0, 1024, dtype=jnp.int32)
    positions = offsets + jnp.arange(SEQ, dtype=jnp.int32)[None, :]
    return {
        "x": x,
        "positions": positions,
        "attn_norm": 1.0 + nrm(ks[2], (DEPTH, D_MODEL), 0.05),
        "w_in": nrm(ks[3], (DEPTH, D_MODEL, IN_WIDTH), D_MODEL ** -0.5),
        "b_gate": nrm(ks[4], (DEPTH, 2 * D_MODEL), 0.1),
        "w_pool": nrm(ks[5], (DEPTH, N_POOL_GROUPS, POOL_GROUP, POOL_GROUP), POOL_GROUP ** -0.5),
        "pool_scale": 1.0 + nrm(ks[6], (DEPTH, POOL_WIDTH), 0.1),
        "q_norm": 1.0 + nrm(ks[7], (DEPTH, HEAD_DIM), 0.05),
        "k_norm": 1.0 + nrm(ks[8], (DEPTH, HEAD_DIM), 0.05),
        "sinks": nrm(ks[9], (DEPTH, N_Q_HEADS), 0.5),
        "w_out": nrm(ks[10], (DEPTH, D_MODEL, D_MODEL), D_MODEL ** -0.5),
        "ffn_norm": 1.0 + nrm(ks[11], (DEPTH, D_MODEL), 0.05),
        "w_up": nrm(ks[12], (DEPTH, D_MODEL, 2 * D_FF), D_MODEL ** -0.5),
        "conv_w": nrm(ks[13], (DEPTH, CONV_WIDTH, 2 * D_FF), CONV_WIDTH ** -0.5),
        "conv_b": nrm(ks[14], (DEPTH, 2 * D_FF), 0.02),
        "w_down": nrm(ks[15], (DEPTH, D_FF, D_MODEL), D_FF ** -0.5),
    }

def second_block(x, positions, attn_norm, w_in, b_gate, w_pool, pool_scale, q_norm, k_norm,
              sinks, w_out, ffn_norm, w_up, conv_w, conv_b, w_down):
    B, S, _ = x.shape
    scale = HEAD_DIM ** -0.5
    for l in range(DEPTH):
        h = rmsnorm_2(x, attn_norm[l])
        z = h @ w_in[l]
        o1 = POOL_WIDTH
        o2 = o1 + Q_WIDTH
        o3 = o2 + KV_WIDTH
        o4 = o3 + KV_WIDTH
        u_pool = z[..., :o1]
        q = z[..., o1:o2].reshape(B, S, N_Q_HEADS, HEAD_DIM)
        k = z[..., o2:o3].reshape(B, S, N_KV_HEADS, HEAD_DIM)
        v = z[..., o3:o4].reshape(B, S, N_KV_HEADS, HEAD_DIM)
        gates = jax.nn.sigmoid((z[..., o4:] + b_gate[l]).astype(jnp.float32)).astype(x.dtype)
        g_pool, g_attn = gates[..., :D_MODEL], gates[..., D_MODEL:]

        a = pool_mixer(u_pool, w_pool[l], pool_scale[l])

        q = partial_rope(rmsnorm_2(q, q_norm[l]), positions) * scale
        k = partial_rope(rmsnorm_2(k, k_norm[l]), positions)
        b = swa_sink_attention(q, k, v, sinks[l])

        x = x + (g_pool * a + g_attn * b) @ w_out[l]

        h = rmsnorm_2(x, ffn_norm[l])
        up = causal_depthwise_conv(h @ w_up[l], conv_w[l], conv_b[l])
        gate, val = up[..., :D_FF], up[..., D_FF:]
        x = x + (jax.nn.silu(gate) * val) @ w_down[l]
    return x


def setup_inputs(seed=0):
    out = dict(first_inputs(seed))
    for name, value in second_inputs(seed + 1).items():
        if name != "x":
            out[name + "_2"] = value
    return out


def reference(
    x, c, ctx, c_ctx, w_ada, b_ada, g_pre_mix, g_post_mix, g_pre_ffn, g_post_ffn, w_in, w_af,
    b_af, w_ab, b_ab, g_head, w_sc, b_sc, w_out, w_up, w_cf, b_cf, w_down, positions_2,
    attn_norm_2, w_in_2, b_gate_2, w_pool_2, pool_scale_2, q_norm_2, k_norm_2, sinks_2, w_out_2,
    ffn_norm_2, w_up_2, conv_w_2, conv_b_2, w_down_2,
):
    x = first_block(
        x, c, ctx, c_ctx, w_ada, b_ada, g_pre_mix, g_post_mix, g_pre_ffn, g_post_ffn, w_in,
        w_af, b_af, w_ab, b_ab, g_head, w_sc, b_sc, w_out, w_up, w_cf, b_cf, w_down,
    )
    return second_block(
        x, positions_2, attn_norm_2, w_in_2, b_gate_2, w_pool_2, pool_scale_2, q_norm_2,
        k_norm_2, sinks_2, w_out_2, ffn_norm_2, w_up_2, conv_w_2, conv_b_2, w_down_2,
    )


_drawn_inputs = setup_inputs


def setup_inputs(seed=0):
    import zlib

    import numpy as np

    out = dict(_drawn_inputs(seed))
    spreads = {}
    factors = {'b_af': 3.888,
     'b_ab': 5.084,
     'g_head': 3.786,
     'b_sc': 8.0,
     'b_cf': 8.0,
     'attn_norm_2': 2.886,
     'b_gate_2': 3.86,
     'q_norm_2': 8.0,
     'k_norm_2': 8.0,
     'sinks_2': 52.571,
     'conv_b_2': 5.133,
     'ffn_norm_2': 3.351}
    for name, (base, spread) in spreads.items():
        noise = np.random.default_rng([zlib.crc32(name.encode()), seed]).standard_normal(out[name].shape)
        drawn = base * np.exp(spread * noise) if base else spread * noise
        out[name] = jnp.asarray(drawn.astype(out[name].dtype))
    for name, factor in factors.items():
        out[name] = (out[name] * factor).astype(out[name].dtype)
    return out
```

```python
import concourse.bass as bass
from concourse import mybir
from contextlib import ExitStack
import numpy as np

F32 = mybir.dt.float32
F32R = mybir.dt.float32r
I32 = mybir.dt.int32
ALU = mybir.AluOpType
ACT = mybir.ActivationFunctionType
AX = mybir.AxisListType

P = 128
D = 1024
T = 512
TC = 256
KT = D // P
EPS = 1e-6
GH, DK, DV = 4, 64, 128
TAU = 16.0
CHUNKS = T // P
ALL_CHUNKS = (T + TC) // P
FF = 2816
FT = FF // P
GRID = 64
ROWS = T // GRID
QH, HD = 16, 64
KV = 2
NQK = QH + KV
HALF_ROPE = 8
BLOCKS = T // P
POOL_WINDOWS = (2, 4, 8, 16)

COL_K, COL_V, COL_AF, COL_Q, COL_OG = 0, 256, 768, 800, 1056
COL_SB, COL_SC, COL_SX = 1568, 2080, 2592
COL2_Q, COL2_KV, COL2_GP, COL2_GA = 1024, 2048, 2304, 3328

PAR = {}
PAR_ROWS = [("b_ada", 48), ("g_pre_mix", 8), ("g_post_mix", 8), ("g_pre_ffn", 8), ("g_post_ffn", 8),
            ("attn_norm_2", 8), ("ffn_norm_2", 8), ("pool_scale_2", 8), ("b_gate_2", 16), ("c", 8),
            ("c_ctx", 8), ("w_sc", 12), ("b_sc", 4), ("b_cf", 22), ("conv_b_2", 44), ("g_head", 1),
            (None, 37), ("w_cf_a", 110), (None, 18), ("w_cf_b", 88), (None, 40),
            ("conv_w_2_a", 88), (None, 40), ("conv_w_2_b", 44)]
_at = 0
for _name, _n in PAR_ROWS:
    if _name:
        PAR[_name] = _at
    _at += _n
PAR_TILES = -(-_at // P)

CONST = {}
CONST_COLS = 0
for _name, _n in [("ident", P), ("upto", P), ("from", P), ("ones", P), ("band", 2 * P), ("sign", 1), ("nsign", 1),
                  ("eps", 1), ("eps4", 1), ("one", 1), ("zero", 1), ("half_pi", 1), ("inv_freq", HALF_ROPE),
                  ("inv_count", 16 * len(POOL_WINDOWS))]:
    CONST[_name] = CONST_COLS
    CONST_COLS += _n
LEVELS = [64, 32, 16, 8, 4, 2, 1]


def shape_constants():
    c = np.zeros((P, CONST_COLS), np.float32)
    put = lambda name, a: c.__setitem__((slice(None), slice(CONST[name], CONST[name] + a.shape[-1])), a)
    i = np.arange(P)
    put("ident", np.eye(P))
    put("upto", (i[:, None] <= i[None, :]) * 1.0)
    put("from", (i[:, None] >= i[None, :]) * 1.0)
    put("ones", np.ones((P, P)))
    k = np.arange(2 * P)
    band = (k[None, :] <= i[:, None] + P) & (i[:, None] + P - k[None, :] < P)
    put("band", np.where(band, 0.0, -1e30))
    s = np.where(i < DK, 1.0 / TAU, -1.0 / TAU)[:, None]
    put("sign", s)
    put("nsign", -s)
    put("eps", np.full((P, 1), EPS))
    put("eps4", np.full((P, 1), 4 * EPS))
    put("one", np.ones((P, 1)))
    put("half_pi", np.full((P, 1), np.pi / 2))
    f = np.float32(500000.0) ** (-np.arange(0, 2 * HALF_ROPE, 2, dtype=np.float32) / np.float32(2 * HALF_ROPE))
    put("inv_freq", np.broadcast_to(f, (P, HALF_ROPE)))
    n = np.stack([1.0 / np.minimum(np.arange(16) + 1.0, w) for w in POOL_WINDOWS]).reshape(1, -1)
    put("inv_count", np.broadcast_to(n, (P, n.size)))
    return c


def shape_masks():
    i = np.arange(P)
    same = lambda n: (i[:, None] // n) == (i[None, :] // n)
    m = [same(2 * h) & ~same(h) for h in LEVELS[1:]] + [np.eye(P, dtype=bool)]
    return np.stack(m, 1).astype(np.int32)


def two_pi_parts():
    rest, parts = 2 * np.pi, []
    for _ in range(3):
        unit = 2.0 ** (np.floor(np.log2(rest)) - 7)
        parts.append(float(np.floor(rest / unit) * unit))
        rest -= parts[-1]
    return parts + [float(np.float32(rest))]


class Order:

    def __init__(self, engine, semaphore):
        self.engine, self.semaphore, self.count, self.loop = engine, semaphore, 0, None

    def done(self, instruction):
        instruction.then_inc(self.semaphore, 1)
        self.count += 1

    def wait(self):
        self.engine.wait_ge(self.semaphore, self.count if self.loop is None else self.loop[0] * self.loop[1] + self.count)

    def start(self, i, per_turn, turns):
        self.loop, self.base, self.turns = (i, per_turn), self.count, turns

    def end(self):
        assert self.count - self.base == self.loop[1], (self.count - self.base, self.loop[1])
        self.count, self.loop = self.base + self.loop[1] * self.turns, None


def build_program(nc, a, out):
    ctx = ExitStack()

    scope = [ctx]

    def sb(name, shape, dt=F32):
        return scope[-1].enter_context(nc.sbuf_tensor(name, shape, dt))

    held = [0]

    def region(kb, *groups):
        made = {}
        for group in groups:
            with ExitStack() as g:
                used = 0
                for name, shape, dt in group:
                    made[name] = g.enter_context(nc.sbuf_tensor(name, shape, dt))
                    used += int(np.prod(shape[1:])) * (1 if dt == mybir.dt.uint8 else 4)
                assert used <= kb * 1024, (group[0][0], used / 1024)
        held[0] += 1
        sb(f"region_{held[0]}", [P, kb * 256])
        return made

    xT = sb("xT", [P, KT, T])
    cst = sb("cst", [P, CONST_COLS])
    masks = sb("masks", [P, len(LEVELS), P], I32)
    par = sb("par", [P, PAR_TILES * P])
    raw = sb("raw", [P, 4, 1024])
    w_hi = sb("w_hi", [P, 2, 1024], F32R)
    w_lo = sb("w_lo", [P, 2, 1024], F32R)
    cond = sb("cond", [P, KT, 2])
    mod = sb("mod", [P, 48, 2])
    scale_in = sb("scale_in", [P, 3, KT])
    gate_out = sb("gate_out", [P, 2, KT])
    dec = sb("dec", [P, GH, ALL_CHUNKS])
    small = sb("small", [P, 96])
    head_norms = sb("head_norms", [P, 2, HD])
    sinks = sb("sinks", [P, QH])
    positions = sb("positions", [P, BLOCKS], I32)
    half_gate_bias = sb("half_gate_bias", [P, 16])
    trig = sb("trig", [P, 6, BLOCKS * HALF_ROPE])
    att_stat = sb("att_stat", [P, 2, 5, QH])

    h_hi, h_lo = sb("h_hi", [P, KT, T], F32R), sb("h_lo", [P, KT, T], F32R)
    N = region(14, [("norm_sq", [P, 2, T], F32), ("norm_acc", [P, T], F32), ("norm_root", [P, T], F32),
                    ("norm_rinv", [P, T], F32), ("norm_t", [P, 2, T], F32)],
               [("g_e", [P, 2, T], F32), ("g_z", [P, 2, T], F32), ("g_att", [P, T], F32), ("g_qe", [P, T], F32),
                ("ada_acc_1", [P, 512], F32)],
               [("kd", [P, BLOCKS, 2 * P], F32), ("v2", [P, BLOCKS, P], F32), ("pt_sb", [P, 2, 512], F32),
                ("o_tok", [P, 2, 512], F32)])
    M = {}
    with ExitStack() as mix1:
        scope.append(mix1)
        M |= region(16, [("hc_hi", [P, KT, TC], F32R), ("hc_lo", [P, KT, TC], F32R)],
                    [("ys_hi", [P, 4, T], F32R), ("ys_lo", [P, 4, T], F32R)])
        M |= region(44, [("ada_first", [P, 5, KT, 2 * P], F32)],
                    [("p1", [P, GH, T], F32), ("p2", [P, GH, T], F32), ("G", [P, ALL_CHUNKS, 512], F32),
                     ("SS", [P, CHUNKS, 512], F32), ("ada", [P, 2, 2, 512], F32)],
                    [("yg_hi", [P, 4, T], F32R), ("yg_lo", [P, 4, T], F32R), ("og", [P, GH, T], F32)])
        M |= region(2, [("rinv_ctx", [P, TC], F32)], [("ada_acc_0", [P, 512], F32)])
        M |= region(24, [("x_tok", [P, ALL_CHUNKS, D], F32)],
                    [("v_tok", [P, ALL_CHUNKS, 512], F32), ("B", [P, GH, T + TC], F32)],
                    [("mo", [P, KT, T], F32)])
        M |= region(8, [("ctxT", [P, KT, TC], F32)], [("k_ctx", [P, GH, TC], F32), ("s_tmp", [P, 512], F32)], [("oT", [P, GH, T], F32)])
        M |= region(6, [("par_rows", [P, PAR_TILES, P], F32)], [("al", [33, T + TC], F32), ("gw", [33, 512], F32)],
                    [("c_sc", [P, T], F32), ("c_p", [P, T], F32), ("c_acc", [P, T], F32)])
        scope.pop()
    with ExitStack() as ffn1:
        scope.append(ffn1)
        M |= region(88, [("f_hi", [P, FT, T], F32R), ("f_lo", [P, FT, T], F32R)], [("mo2", [P, T], F32)],
                    [("result", [P, BLOCKS, D], F32)])
        M |= region(8, [("f_acc", [P, 2, T], F32), ("f_act", [P, 2, T], F32)])
        scope.pop()
    with ExitStack() as mix2:
        scope.append(mix2)
        M |= region(32, [("pl_hi", [P, KT, T], F32R), ("pl_lo", [P, KT, T], F32R)],
                    [("y2_hi", [P, KT, T], F32R), ("y2_lo", [P, KT, T], F32R)])
        M |= region(16, [("ya", [P, KT, T], F32)])
        M |= region(20, [("qkv", [P, BLOCKS, 1152], F32)], [("ga", [P, KT, T], F32)])
        M |= region(20, [("squares2", [P, BLOCKS, NQK * HD], F32)], [("qT", [P, KT, T], F32), ("kT", [P, KV, T], F32)])
        M |= region(8, [("rot", [P, 2, BLOCKS * NQK * HALF_ROPE], F32)], [("pw", [P, 4, T], F32)],
                    [("scores_sb", [P, 8, 2 * P], F32)])
        scope.pop()
    sb("region_mixers_and_ffn", [P, 96 * 256])
    norm_sq, norm_acc, norm_root, norm_rinv, norm_t, g_e, g_z, g_att, g_qe, ada_acc_1, kd, v2, pt_sb, o_tok = N.values()
    hc_hi, hc_lo, ys_hi, ys_lo, p1, p2, yg_hi, yg_lo = (M[k] for k in (
        "hc_hi", "hc_lo", "ys_hi", "ys_lo", "p1", "p2", "yg_hi", "yg_lo"))
    x_tok, v_tok, B, mo, G, og, SS, ctxT, k_ctx, s_tmp, oT, ada = (M[k] for k in (
        "x_tok", "v_tok", "B", "mo", "G", "og", "SS", "ctxT", "k_ctx", "s_tmp", "oT", "ada"))
    ada_first, rinv_ctx = M["ada_first"], M["rinv_ctx"]
    ada_acc = (M["ada_acc_0"], ada_acc_1)
    par_rows, al, gw, c_sc, c_p, c_acc = (M[k] for k in ("par_rows", "al", "gw", "c_sc", "c_p", "c_acc"))
    f_hi, f_lo, mo2, f_acc, f_act = (M[k] for k in ("f_hi", "f_lo", "mo2", "f_acc", "f_act"))
    pl_hi, pl_lo, y2_hi, y2_lo, ya, qkv, ga, squares2, qT, kT, pw, rot, scores_sb, result = (M[k] for k in (
        "pl_hi", "pl_lo", "y2_hi", "y2_lo", "ya", "qkv", "ga", "squares2", "qT", "kT", "pw", "rot", "scores_sb", "result"))
    ps = ctx.enter_context(nc.psum_tensor("ps", [P, 8, 512], F32))

    def const(name, n=1, rows=P):
        return cst[0:rows, CONST[name]:CONST[name] + n]

    def column(name, i=0, n=1):
        return par[:, bass.ds(PAR[name] + i, n)]

    LV = len(LEVELS)

    def taken(step):
        return 2 * step + 2 + (step + 1) // LV

    STATE_ORDER = [CHUNKS, CHUNKS + 1, 0, 1, 2, 3]

    row = lambda name: a[name].rearrange("(r p) -> r p", p=P)
    PAR_LOADS = [(n, 0, c, row(n)) for n, c in PAR_ROWS if n and n[:-2] not in ("w_cf", "conv_w_2")]
    PAR_LOADS += [("w_cf_a", 0, 110, row("w_cf")[0:110, :]), ("w_cf_b", 0, 88, row("w_cf")[110:198, :]),
                  ("conv_w_2_a", 0, 88, row("conv_w_2")[0:88, :]), ("conv_w_2_b", 0, 44, row("conv_w_2")[88:132, :])]
    PAR_DMAS = len(PAR_LOADS)

    sems = {}

    def S(name):
        if name not in sems:
            sems[name] = ctx.enter_context(nc.semaphore(name))
        return sems[name]

    def columns(w, first):
        return lambda i: (w[0:D, bass.ds(first + P * i, P)].rearrange("(k p) m -> p k m", p=P), KT)

    def rows(w, first, n):
        return lambda i: (w[bass.ds(i * (n * P), n * P), first:first + 1024 // n].rearrange("(k p) m -> p k m", p=P), n)

    def quarters(w, first):
        return lambda i: (w[first:first + 4 * P, bass.ds(256 * i, 256)].rearrange("(k p) m -> p k m", p=P), 4)

    w_in, w_in2 = a["w_in"], a["w_in_2"]
    EARLY = 6
    PHASES = [
        ("low", 1, 1, columns(w_in, COL_AF)), ("k", 2, 1, columns(w_in, COL_K)), ("q", 2, 1, columns(w_in, COL_Q)),
        ("v", 4, 1, rows(w_in, COL_V, 2)),
        ("branch", 16, 4, [columns(w_in, c) for c in (COL_OG, COL_SB, COL_SC, COL_SX)]),
        ("out_s", 4, 1, quarters(a["w_out"], 4 * P)), ("out_g", 4, 1, quarters(a["w_out"], 0)),
        ("up", 44, 2, [columns(a["w_up"], 0), columns(a["w_up"], FF)]),
        ("down", 22, 1, rows(a["w_down"], 0, 1)),
        ("q2a", 4, 1, rows(w_in2, COL2_Q, 2)), ("q2b", 4, 1, rows(w_in2, COL2_Q + 512, 2)),
        ("kv2", 2, 1, rows(w_in2, COL2_KV, 4)),
        ("pool", 4, 1, columns(w_in2, 0)), ("gp_first", 2, 1, columns(w_in2, COL2_GP)),
        ("pool_late", 4, 1, columns(w_in2, 4 * P)), ("gp_early", EARLY - 2, 1, columns(w_in2, COL2_GP + 2 * P)),
        ("wpool", 2, 1, rows(a["w_pool_2"], 0, 4)), ("gp", 8 - EARLY, 1, columns(w_in2, COL2_GP + EARLY * P)),
        ("ga", 8, 1, columns(w_in2, COL2_GA)),
        ("out2", 8, 1, columns(a["w_out_2"], 0)),
        ("up2", 44, 2, [columns(a["w_up_2"], 0), columns(a["w_up_2"], FF)]),
        ("down2", 22, 1, rows(a["w_down_2"], 0, 1)),
    ]
    FIRST, at = {}, 0
    for name, n, _, _ in PHASES:
        FIRST[name] = at
        at += n
    UNITS = at
    ADA_PAIRS, FIRST_SLOTS = 8, 5
    ADA_PIECES = 32
    raw_loaded = [S(f"raw_loaded_{s}") for s in range(4)]
    ada_first_loaded = [S(f"ada_first_loaded_{s}") for s in range(FIRST_SLOTS)]
    PIECE_SLOTS = 5
    ada_loaded = [S(f"ada_loaded_{s}") for s in range(PIECE_SLOTS)]

    def ada_slot(n):
        s = n % PIECE_SLOTS
        return ada[:, s, :, :] if s < 2 else v_tok[:, 2 * (s - 2):2 * (s - 2) + 2, :]

    def pieces_after(u):
        return range(0, PIECE_SLOTS) if u == 3 else range(min(4 * u - 11, ADA_PIECES), min(4 * u - 7, ADA_PIECES)) if u > 3 else ()

    def load_par_rows(engine, half):
        engine.wait_ge(S("rows_cleared"), 1)
        for name, first, n, src in PAR_LOADS[half::2]:
            r = PAR[name] + first
            engine.dma_start(par_rows[r % P:r % P + n, r // P, :], src).then_inc(S("par_loaded"), 16)

    def out_ready(m):
        return (S("units_done"), FIRST["out_g"] + m // 2 + 1) if m % 2 else (S("out_done"), m // 2 + 1)

    def gate_unit(s):
        return FIRST["gp_first"] + s if s < 2 else FIRST["gp_early"] + s - 2 if s < EARLY else FIRST["gp"] + s - EARLY

    def pool_unit(p):
        return FIRST["pool"] + p if p < 4 else FIRST["pool_late"] + p - 4

    def gate_parts(s):
        return [(EARLY + i // 3, i % 3) for i in (2 * s, 2 * s + 1) if i < 3 * (16 - EARLY)]

    def gate_done_in(s):
        return next((tile for tile, part in gate_parts(s) if part == 2), None)

    def x_done(r, m):
        if r < 2:
            return (S("x_ready_pool" if m % 2 else "x_ready"), KT // 2 * r + m // 2 + 1)
        return S("x_ready"), KT + m + 1

    def h_done(i, m):
        if i < 2:
            return S("h_ready"), KT * i + m + 1
        half = KT // 2 * (i - 2) + m // 2 + 1
        return (S("h_ready_pool"), half) if m % 2 else (S("h_ready"), 2 * KT + half)

    def normed(m):
        return (norm_t, norm_sq)[(m // 2) % 2][:, m % 2, :]

    block = ctx.enter_context(nc.Block())

    @block.sync
    def _(sp):
        def load_unit(u, slot, source):
            src, n = source
            if not isinstance(u, int) or u >= 4:
                sp.wait_ge(S("lo_split"), u - 3)
            sp.dma_start(raw[:, slot, :].rearrange("p (k m) -> p k m", k=n), src).then_inc(raw_loaded[slot], 16)

        def load_ada(n):
            if n >= PIECE_SLOTS:
                sp.wait_ge(S("ada_added"), 2 * (n - PIECE_SLOTS) + 2)
            chunk, k = n // 4, 2 * (n % 4)
            sp.dma_start(ada_slot(n), a["w_ada"][k * P:(k + 2) * P, 2048 + 512 * chunk:2560 + 512 * chunk]
                         .rearrange("(k p) m -> p k m", p=P)).then_inc(ada_loaded[n % PIECE_SLOTS], 16)

        for i in range(2):
            sp.dma_start(x_tok[:, 0:CHUNKS, 512 * i:512 * i + 512],
                         a["x"][:, 512 * i:512 * i + 512].rearrange("(t p) d -> p t d", p=P)).then_inc(S(f"x_loaded_{i}"), 16)
        sp.dma_start(x_tok[:, CHUNKS:, :], a["ctx"].rearrange("(t p) d -> p t d", p=P)).then_inc(S("ctx_loaded"), 16)
        load_par_rows(sp, 1)
        for n in range(ADA_PAIRS):
            if n >= FIRST_SLOTS:
                sp.wait_ge(S("ada_first_used"), n - FIRST_SLOTS + 1)
            sp.dma_start(ada_first[:, n % FIRST_SLOTS, :, :], a["w_ada"][:, n * 2 * P:(n + 1) * 2 * P]
                         .rearrange("(k p) m -> p k m", p=P)).then_inc(ada_first_loaded[n % FIRST_SLOTS], 16)
        for name, n, period, source in PHASES:
            u0 = FIRST[name]

            def cut(turn, r):
                if period == 1:
                    return source(turn * 4 + r)
                return source[r % period](turn * (4 // period) + r // period)

            if u0 + n <= FIRST["out_s"]:
                for i in range(n):
                    load_unit(u0 + i, (u0 + i) % 4, cut(i // 4, i % 4))
                    if u0 + i == 3:
                        sp.wait_ge(S("ada_turned"), 1)
                    for n_piece in pieces_after(u0 + i):
                        load_ada(n_piece)
                continue
            if n >= 8:
                with sp.Fori(0, n // 4) as turn:
                    for r in range(4):
                        load_unit(turn * 4 + (u0 + r), (u0 + r) % 4, cut(turn, r))
            for i in range(n - n % 4 if n >= 8 else 0, n):
                load_unit(u0 + i, (u0 + i) % 4, cut(i // 4, i % 4))
        for n in range(2 * BLOCKS):
            half, t = n // BLOCKS, n % BLOCKS
            sp.wait_ge(S("result_copied"), n + 1)
            cols = slice(512 * half, 512 * half + 512)
            sp.dma_start(out[t * P:(t + 1) * P, cols], result[:, t, cols]).then_inc(S("stored"), 16)
        sp.wait_ge(S("stored"), 16 * 2 * BLOCKS)

    @block.gpsimd
    def _(pool):
        HEAD_COLUMNS = 16

        def split(u, slot, loads):
            pool.wait_ge(raw_loaded[slot], loads)
            if not isinstance(u, int) or u >= 2:
                pool.wait_ge(S("units_done"), u - 1)
            few = raw[:, slot, 0:HEAD_COLUMNS]
            pool.tensor_tensor(w_hi[:, slot % 2, 0:HEAD_COLUMNS], few, const("ones", HEAD_COLUMNS), ALU.mult).then_inc(S("hi_split"), 1)
            pool.tensor_scalar(w_hi[:, slot % 2, HEAD_COLUMNS:], raw[:, slot, HEAD_COLUMNS:], 1.0, 0.0, ALU.mult, ALU.add)\
                .then_inc(S("hi_split"), 1)
            pool.wait_ge(S("hi_split"), u * 2 + 2)
            pool.tensor_tensor(w_lo[:, slot % 2, :], raw[:, slot, :], w_hi[:, slot % 2, :].bitcast(F32),
                               ALU.subtract).then_inc(S("lo_split"), 1)

        pool.wait_ge(S("consts_loaded"), 16)
        def stream(first, end):
            turns = (end - first) // 4
            with pool.Fori(0, turns) as turn:
                for u in range(first, first + 4):
                    split(turn * 4 + u, u % 4, turn * 16 + 16 * (u // 4 + 1))
            for u in range(first + 4 * turns, end):
                split(u, u % 4, 16 * (u // 4 + 1))

        def residual_odd(r):
            for m in range(1, KT, 2):
                pool.wait_ge(S("branch_normed"), KT * r + m + 1)
                pool.tensor_tensor(xT[:, m, :], xT[:, m, :], norm_t[:, 1, :], ALU.add).then_inc(S("x_ready_pool"), 1)

        def low_odd(i):
            for m in range(1, KT, 2):
                if i == 2:
                    pool.wait_ge(S("shifted"), m // 2 + 1)
                else:
                    pool.wait_ge(S("h_hi_ready"), KT * i + m + 1)
                pool.tensor_tensor(h_lo[:, m, :], normed(m), h_hi[:, m, :].bitcast(F32), ALU.subtract)\
                    .then_inc(S("h_ready_pool"), 1)

        for u in range(4):
            split(u, u, 16)
        stream(4, FIRST["up"] + 2)
        residual_odd(0)
        low_odd(2)
        stream(FIRST["up"] + 2, FIRST["q2a"] + 2)
        residual_odd(1)
        low_odd(3)
        stream(FIRST["q2a"] + 2, FIRST["up2"] + 2)
        low_odd(4)
        stream(FIRST["up2"] + 2, UNITS)

    @block.tensor
    def _(pe):
        def triple(dst, lhs_hi, lhs_lo, rhs_hi, rhs_lo, first, last):
            nc.tensor.matmul(dst, lhs_hi, rhs_hi, start=first, stop=False)
            nc.tensor.matmul(dst, lhs_hi, rhs_lo, start=False, stop=False)
            return nc.tensor.matmul(dst, lhs_lo, rhs_hi, start=False, stop=last)

        def wait_unit(u):
            pe.wait_ge(S("lo_split"), u + 1)

        def channels(dst, slot, hi, lo, tiles=range(KT), first=0, last=KT - 1):
            for k in tiles:
                mm = triple(dst, w_hi[:, slot, k * P:(k + 1) * P], w_lo[:, slot, k * P:(k + 1) * P],
                            hi[:, k, :], lo[:, k, :], k == first, k == last)
            return mm

        def tokens(dst, slot, hi, lo, k, k_unit, width, t, first, last):
            return triple(dst, hi[:, k, t * P:(t + 1) * P], lo[:, k, t * P:(t + 1) * P],
                          w_hi[:, slot, k_unit * width:(k_unit + 1) * width],
                          w_lo[:, slot, k_unit * width:(k_unit + 1) * width], first, last)

        def two_units(u, i, banks):
            wait_unit(u)
            for at in range(KT + 4):
                for n in range(2):
                    k = at - 4 * n
                    if at >= 8 and n == 0 or k < 0 or k >= KT:
                        continue
                    if n == 0:
                        pe.wait_ge(*h_done(i, k))
                    elif k == 0:
                        wait_unit(u + 1)
                    mm = channels(ps[:, banks[n], :], (u + n) % 2, h_hi, h_lo, [k])
                    if k == KT - 1:
                        yield mm

        def ada_pair(n):
            pe.wait_ge(ada_first_loaded[n % FIRST_SLOTS], 16 * (n // FIRST_SLOTS + 1))
            for t in range(KT):
                mm = nc.tensor.matmul(ps[0:2, 2 + n // 2, (n % 2) * 256:(n % 2) * 256 + 256], cond[:, t, :],
                                      ada_first[:, n % FIRST_SLOTS, t, :], start=(t == 0), stop=(t == KT - 1))
            mm.then_inc(S("ada_first_used"), 1)

        def ada_sum(chunk):
            pe.wait_ge(S("ada_added"), 8 * chunk + 8)
            if chunk == 0:
                pe.wait_ge(S("proj_copied"), 8)
            for i in range(4):
                mm = nc.tensor.matmul(ps[:, 1, 4 * chunk + i:4 * chunk + i + 1], ada_acc[chunk % 2][:, i * P:(i + 1) * P],
                                      const("ones"), start=True, stop=True)
            mm.then_inc(S("ada_out"), 1)

        def sum_squares(k, n):
            pe.wait_ge(S("norm_added"), 7 * k + 7)
            if k >= 1:
                pe.wait_ge(S("norm_rooted"), k)
            nc.tensor.matmul(ps[:, 7, 0:n], const("ones", P), norm_acc[:, 0:n], start=True, stop=True).then_inc(S("norm_ss"), 1)

        def sum_tiles(k, bank_free):
            pe.wait_ge(S("norm_rooted"), k)
            for m in range(KT):
                pe.wait_ge(S("norm_squared"), KT * k + m + 1)
                if m == 0 and bank_free:
                    pe.wait_ge(*bank_free)
                nc.tensor.matmul(ps[:, 7, :], const("ones", P), norm_sq[:, m % 2, :], start=(m == 0), stop=(m == KT - 1))\
                    .then_inc(S("norm_ss" if m == KT - 1 else "square_used"), 1)

        pe.wait_ge(S("consts_loaded"), 16)
        for n in range(14):
            if n in (0, 4):
                pe.wait_ge(S(f"x_loaded_{n // 4}"), 16)
            elif n == 8:
                pe.wait_ge(S("par_loaded"), PAR_DMAS * 16)
            elif n == 10:
                pe.wait_ge(S("ctx_loaded"), 16)
            if n >= 6:
                pe.wait_ge(S("turned_out"), n - 5)
            for r in range(4):
                if n < 8:
                    src = x_tok[:, r, n * P:(n + 1) * P]
                elif n < 10:
                    if r == 3:
                        continue
                    src = par_rows[:, 3 * (n - 8) + r, :]
                else:
                    k = 2 * (n - 10) + r // 2
                    src = x_tok[:, CHUNKS + r % 2, k * P:(k + 1) * P]
                mm = nc.tensor.transpose(ps[:, n % 6, r * P:(r + 1) * P], src, const("ident", P))
            mm.then_inc(S("turned"), 1)
        pe.wait_ge(S("cond_ready"), 2)
        pe.wait_ge(S("turned_out"), 14)
        for n in range(ADA_PAIRS):
            ada_pair(n)
            if n == 1:
                sum_squares(0, T)
            elif n == 3:
                sum_squares(1, TC)
        for m in range(16):
            if m % 4 == 0:
                pe.wait_ge(S("ada_rows"), m // 4 + 1)
            mm = nc.tensor.matmul(ps[:, 6, 2 * m:2 * m + 2], v_tok[0:2, m // 4, (m % 4) * P:(m % 4 + 1) * P],
                                  cst[0:2, CONST["ident"]:CONST["ident"] + 2], start=True, stop=True)
        mm.then_inc(S("ada_turned"), 1)

        def gates(c):
            if c == 0:
                pe.wait_ge(S("low_copied"), 2)
                pe.wait_ge(S("gw_loaded"), 64)
            if c >= 2:
                pe.wait_ge(S("gate_min"), c - 1)
            nc.tensor.matmul(ps[:, 4 + c % 2, :], al[:, c * P:(c + 1) * P], gw[:, :], start=True, stop=True)\
                .then_inc(S("gates_mm"), 1)

        def sums(c):
            pe.wait_ge(S("gate_done"), 1 + c // 3)
            if c >= 1:
                pe.wait_ge(S("sums_copied"), c)
            else:
                pe.wait_ge(S("proj_copied"), 7)
            for h in range(GH):
                for d, way in ((0, "upto"), (1, "from")):
                    mm = nc.tensor.matmul(ps[d * DK:(d + 1) * DK, 0, h * P:(h + 1) * P],
                                          G[:, c, h * P + d * DK:h * P + (d + 1) * DK], const(way, P), start=True, stop=True)
            mm.then_inc(S("sums_mm"), 1)

        def of_ctx(u, bank):
            for k in range(KT):
                if u == 0:
                    pe.wait_ge(*h_done(1, k))
                mm = channels(ps[:, bank, 0:TC], u % 2, hc_hi, hc_lo, [k])
            mm.then_inc(S("units_done"), 1)

        pe.wait_ge(S("turned_out"), 14)
        for _ in two_units(0, 0, (0, 2)):
            pass
        of_ctx(0, 1)
        of_ctx(1, 3)
        for c in range(3):
            gates(c)
        wait_unit(2)
        channels(ps[:, 0, :], 0, h_hi, h_lo)
        of_ctx(2, 1)
        for c in range(3, ALL_CHUNKS):
            gates(c)
        pe.wait_ge(S("mod_ready"), 1)
        pe.wait_ge(S("norm_rooted"), 2)
        for u in (3, 4):
            wait_unit(u)
            channels(ps[:, 3 + u, :], u % 2, h_hi, h_lo).then_inc(S("units_done"), 1)
            ada_sum(u - 3)
        pe.wait_ge(S("gate_min"), ALL_CHUNKS)
        for i in range(4):
            u = FIRST["v"] + i
            wait_unit(u)
            for kk in range(2):
                k = 2 * i + kk
                for t in range(ALL_CHUNKS):
                    if i == kk == 0 and t in (0, 4):
                        pe.wait_ge(S("proj_copied"), 4 if t == 0 else 12)
                    hi, lo, tt = (h_hi, h_lo, t) if t < CHUNKS else (hc_hi, hc_lo, t - CHUNKS)
                    mm = tokens(ps[:, 2 + t, :], u % 2, hi, lo, k, kk, 512, tt, k == 0, k == KT - 1)
                if kk == 1:
                    mm.then_inc(S("units_done"), 1)
                if 2 <= k < 8:
                    sums(k - 2)
                    ada_sum(k)

        def branch(tile, part):
            n, half = part // 2, part % 2
            u = FIRST["branch"] + 4 * tile + n
            if half == 0:
                wait_unit(u)
                if tile >= 1:
                    pe.wait_ge(S("branch_act" if n == 2 else "branch_dve"), (3 * tile, 3 * tile, 2 * tile, 3 * tile - 2)[n] - (n == 0))
                elif n == 0:
                    pe.wait_ge(S("sums_copied"), ALL_CHUNKS)
                elif n == 1:
                    pe.wait_ge(S("mod_ready"), 2)
                elif n == 2:
                    pe.wait_ge(S("v_copied"), 2)
            mm = channels(ps[:, n, :], u % 2, h_hi, h_lo, range(4 * half, 4 * half + 4))
            if half:
                mm.then_inc(S("units_done"), 1)

        def turn_keys(n):
            pe.wait_ge(S("ke_ready"), n + 1)
            if n >= 2:
                pe.wait_ge(S("ket_copied"), n - 1)
            for h in range(GH):
                mm = nc.tensor.transpose(ps[:, 4 + 3 * (n % 2), h * P:(h + 1) * P], g_z[:, n % 2, h * P:(h + 1) * P],
                                         const("ident", P))
            mm.then_inc(S("ke_turned"), 1)

        def states(n, c):
            pe.wait_ge(S("ket_copied"), n + 1)
            if n >= 1:
                pe.wait_ge(S("state_read"), n)
            keys = (g_qe, g_att)[n % 2]
            for h in range(GH):
                mm = nc.tensor.matmul(ps[:, 5, h * P:(h + 1) * P], keys[:, h * P:(h + 1) * P],
                                      v_tok[:, c, h * P:(h + 1) * P], start=True, stop=True)
            mm.then_inc(S("state_mm"), 1)

        branch(0, 0)
        branch(0, 1)
        pe.wait_ge(S("v_copied"), ALL_CHUNKS)
        turn_keys(0)
        for n, c in enumerate(STATE_ORDER):
            if n + 1 < ALL_CHUNKS:
                turn_keys(n + 1)
            states(n, c)
            branch(0, n + 2)

        def level(c, n):
            step = LV * c + n
            z = g_z[:, step % 2, :].rearrange("p (h t) -> p h t", h=GH)
            half = LEVELS[n]
            pe.wait_ge(S("z_ready"), 2 * step + 2)
            if step >= 1:
                pe.wait_ge(S("att_taken"), taken(step - 1))
            else:
                pe.wait_ge(S("state_read"), ALL_CHUNKS)
            for bank, at, half_at in ((4, 0, 1), (5, DK, 0)):
                for h in range(GH):
                    zh = z[at:at + DK, h, :]
                    rhs = zh.rearrange("p (b s t) -> p b s t", s=2, t=half)[:, :, half_at, :]
                    mm = nc.tensor.matmul(ps[:, bank, h * 64:(h + 1) * 64], zh, rhs, start=True, stop=True)
            mm.then_inc(S("level_mm"), 1)

        def diagonal(c):
            if c >= 1:
                pe.wait_ge(S("o_rooted"), c)
            for h in range(GH):
                mm = nc.tensor.matmul(ps[:, 6, h * P:(h + 1) * P], p2[0:DK, h, c * P:(c + 1) * P],
                                      p1[0:DK, h, c * P:(c + 1) * P], start=True, stop=True)
            mm.then_inc(S("diag_mm"), 1)

        def outputs(c):
            pe.wait_ge(S("att_taken"), taken(LV * c + LV - 1))
            pe.wait_ge(S("qe_ready"), 2 * (c + 1))
            pe.wait_ge(S("states_done"), CHUNKS)
            for h in range(GH):
                cols = slice(h * P, (h + 1) * P)
                nc.tensor.matmul(ps[:, 6, cols], v_tok[:, c, cols], g_att[:, cols], start=True, stop=False)
                mm = nc.tensor.matmul(ps[:, 6, cols], SS[:, c, cols], g_qe[:, cols], start=False, stop=True)
            mm.then_inc(S("outputs_mm"), 1)

        def head_sums(c):
            pe.wait_ge(S("o_squared"), c + 1)
            nc.tensor.matmul(ps[:, 6, :], const("ones", P), c_sc[:, :], start=True, stop=True).then_inc(S("o_ss"), 1)

        def out_tile(name, m, hi, lo, ready):
            u = FIRST[name] + m // 2
            first = name == "out_s"
            if m % 2 == 0:
                wait_unit(u)
            for k in range(4):
                if m == 0:
                    pe.wait_ge(S("y_ready"), ready + k + 1)
                at = k * 256 + (m % 2) * P
                mm = triple(ps[:, (m + 7) % 8, :], w_hi[:, u % 2, at:at + P], w_lo[:, u % 2, at:at + P],
                            hi[:, k, :], lo[:, k, :], first and k == 0, not first and k == 3)
            if m % 2:
                mm.then_inc(S("units_done"), 1)
            elif not first:
                mm.then_inc(S("out_done"), 1)

        for c in range(CHUNKS):
            for n in range(LV):
                level(c, n)
                if c < CHUNKS - 1:
                    branch(c + 1, n)
                elif n >= 2:
                    if n == 2:
                        pe.wait_ge(S("branch_act"), 2 * CHUNKS)
                        pe.wait_ge(S("branch_dve"), 3 * CHUNKS)
                    out_tile("out_s", n - 2, ys_hi, ys_lo, 0)
                if n == 1 and c >= 1:
                    head_sums(c - 1)
                if n == 4:
                    diagonal(c)
            if c < CHUNKS - 1:
                branch(c + 1, 7)
            outputs(c)
        out_tile("out_s", 5, ys_hi, ys_lo, 0)
        head_sums(CHUNKS - 1)
        out_tile("out_s", 6, ys_hi, ys_lo, 0)
        pe.wait_ge(S("o_rooted"), CHUNKS)
        out_tile("out_s", 7, ys_hi, ys_lo, 0)
        for m in range(KT):
            out_tile("out_g", m, yg_hi, yg_lo, 4)
        pe.wait_ge(S("mo_copied"), 1)
        sum_squares(2, T)
        sum_tiles(3, None)

        def ffn(i, up, down, modulation):
            base, f = FT * i, FIRST[up]
            for mm in two_units(f, modulation, (0, 1)):
                mm.then_inc(S("units_done"), 1)
            for r in (2, 3):
                wait_unit(f + r)
                channels(ps[:, r, :], (f + r) % 2, h_hi, h_lo).then_inc(S("units_done"), 1)
            with pe.Fori(1, FT // 2) as turn:
                for r in range(4):
                    pe.wait_ge(S("lo_split"), turn * 4 + (f + r + 1))
                    pe.wait_ge(S("taps_done" if r % 2 == 0 else "gated"), turn * 2 + (base - 1 + r // 2))
                    channels(ps[:, r, :], (f + r) % 2, h_hi, h_lo).then_inc(S("units_done"), 1)

            g = FIRST[down]

            def down_tile(j, slot, m, first, last):
                one = lambda t: t[:, j, :] if isinstance(j, int) else t[:, bass.ds(j, 1), :].rearrange("p a t -> p (a t)")
                return triple(ps[:, (m + 7) % 8, :], w_hi[:, slot, m * P:(m + 1) * P], w_lo[:, slot, m * P:(m + 1) * P],
                              one(f_hi), one(f_lo), first, last)

            for tiles in ((5, 6, 7, 0, 1, 2), (3, 4)):
                for j in range(2):
                    for m in tiles:
                        if tiles[0] == 5 and m == 5:
                            wait_unit(g + j)
                            pe.wait_ge(S("f_ready"), 2 + base + j + 1)
                        if j == 0 and m in (1, 3):
                            pe.wait_ge(S("taps_done"), base + FT - (m == 1))
                            pe.wait_ge(S("gated"), base + FT - (m == 1))
                        mm = down_tile(j, (g + j) % 2, m, j == 0, False)
                    if tiles[0] == 3:
                        mm.then_inc(S("units_done"), 1)
            with pe.Fori(0, FT // 2 - 2) as turn:
                for r in range(2):
                    pe.wait_ge(S("lo_split"), turn * 2 + (g + r + 3))
                    pe.wait_ge(S("f_ready"), turn * 2 + (2 + base + r + 3))
                    for m in range(KT):
                        mm = down_tile(turn * 2 + (r + 2), (g + r) % 2, m, False, False)
                    mm.then_inc(S("units_done"), 1)
            wait_unit(g + FT - 2)
            pe.wait_ge(S("f_ready"), 2 + base + FT - 1)
            for m in range(KT):
                mm = down_tile(FT - 2, (g + FT - 2) % 2, m, False, False)
            mm.then_inc(S("units_done"), 1)
            wait_unit(g + FT - 1)
            pe.wait_ge(S("f_ready"), 2 + base + FT)
            for m in range(KT):
                down_tile(FT - 1, (g + FT - 1) % 2, m, False, True)\
                    .then_inc(S("units_done" if m == KT - 1 else "down_done"), 1)

        ffn(0, "up", "down", 2)
        sum_tiles(4, (S("mo_copied"), 2))
        sum_tiles(5, None)

        def token_units(name, n_k, width, bank, first_wait):
            for i in range(KT // n_k):
                u = FIRST[name] + i
                wait_unit(u)
                for kk in range(n_k):
                    k = n_k * i + kk
                    if first_wait:
                        pe.wait_ge(*h_done(3, k))
                    for t in range(BLOCKS):
                        mm = tokens(ps[:, bank + t, 0:width], u % 2, h_hi, h_lo, k, kk, width, t, k == 0, k == KT - 1)
                mm.then_inc(S("units_done"), 1)

        token_units("q2a", 2, 512, 0, True)
        pe.wait_ge(S("norm_rooted"), 6)
        token_units("q2b", 2, 512, 4, False)
        pe.wait_ge(S("qkv_copied"), 4)
        token_units("kv2", 4, 256, 0, False)
        def gate_part(s, part):
            u = gate_unit(s)
            if part == 0:
                wait_unit(u)
                if s < 2:
                    pe.wait_ge(S("qkv_copied"), 16)
                else:
                    pe.wait_ge(S("gate_tanh"), s - 1)
            mm = channels(ps[:, s % 2, :], u % 2, h_hi, h_lo, (range(3), range(3, 6), range(6, 8))[part])
            if part == 2:
                mm.then_inc(S("units_done"), 1)

        for p in range(8):
            u = pool_unit(p)
            wait_unit(u)
            pe.wait_ge(S("qkv_copied"), 5 + p if p < 4 else 8)
            if p >= 4:
                pe.wait_ge(S("pool_copied"), p - 3)
            channels(ps[:, 4 + p % 4, :], u % 2, h_hi, h_lo).then_inc(S("units_done"), 1)
            if p == 3:
                for s in range(2):
                    for part in range(3):
                        gate_part(s, part)

        for s in range(1, EARLY):
            for part in range(3) if s > 1 else ():
                gate_part(s, part)
            for n in (2 * s - 2, 2 * s - 1):
                if n == 0:
                    pe.wait_ge(S("qkv_copied"), 16)
                    pe.wait_ge(S("qk_ready"), 1)
                elif n >= 2:
                    pe.wait_ge(S("qT_copied"), n - 1)
                if n == 8:
                    pe.wait_ge(S("kd_ready"), 1)
                for r in range(4):
                    src = qkv[:, n // 2, (4 * (n % 2) + r) * P:(4 * (n % 2) + r + 1) * P] if n < 8 else \
                        kd[:, r, (n - 8) * P:(n - 7) * P]
                    mm = nc.tensor.transpose(ps[:, 2 + n % 2, r * P:(r + 1) * P], src, const("ident", P))
                mm.then_inc(S("q_turned"), 1)

        pe.wait_ge(S("pool_copied"), 8)
        for i in range(2):
            u = FIRST["wpool"] + i
            wait_unit(u)
            for n in range(4):
                g, m = 2 * i + n // 2, n % 2
                if i == 1:
                    pe.wait_ge(S("ya_ready"), n + 1)
                pe.wait_ge(S("pl_ready"), 2 * g + 2)
                for kk in range(2):
                    at = ((g % 2) * 2 + kk) * 256 + m * P
                    mm = triple(ps[:, 4 + n, :], w_hi[:, u % 2, at:at + P], w_lo[:, u % 2, at:at + P],
                                pl_hi[:, 2 * g + kk, :], pl_lo[:, 2 * g + kk, :], kk == 0, kk == 1)
                mm.then_inc(S("units_done" if n == 3 else "mixed"), 1)

        def halves(n):
            return (0, 1) if n else (1,)

        def scores(s):
            n, g = s // 4, s % 4
            if s == 0:
                pe.wait_ge(S("qT_copied"), 10)
            else:
                pe.wait_ge(S("scores_taken"), 4 * s)
            first = (n - 1 if n else 0) * P
            for i in range(4):
                h = 4 * g + i
                rows = slice((h % 2) * HD, (h % 2) * HD + HD)
                dst = ps[:, 2 + i % 2, (i // 2) * 256 + (0 if n else P):(i // 2) * 256 + 256]
                mm = nc.tensor.matmul(dst, qT[rows, h // 2, n * P:(n + 1) * P], kT[rows, h // 8, first:(n + 1) * P],
                                      start=True, stop=True)
            mm.then_inc(S("scores_mm"), 1)

        def turn_probs(s):
            n = s // 4
            pe.wait_ge(S("probs_ready"), 4 * s + 4)
            if s >= 1:
                pe.wait_ge(S("pt_copied"), 2 * s)
            if n >= 1:
                pe.wait_ge(S("bT_copied"), 2 * n)
            if s == 0:
                pe.wait_ge(S("ya_ready"), 8)
            for i in range(4):
                for half in halves(n):
                    at = (i % 2) * 256 + half * P
                    mm = nc.tensor.transpose(ps[:, 4 + i // 2, at:at + P],
                                             scores_sb[:, (s % 2) * 4 + i, half * P:(half + 1) * P], const("ident", P))
                if i % 2:
                    mm.then_inc(S("probs_turned"), 1)

        def weigh(s):
            n, g = s // 4, s % 4
            pe.wait_ge(S("pt_copied"), 2 * s + 2)
            if g % 2 == 0 and n >= 1:
                pe.wait_ge(S("o_tok_ready"), 2 * (n - 1) + 1 + g // 2)
            for i in range(4):
                h = 4 * g + i
                for half in halves(n):
                    at = (i % 2) * 256 + half * P
                    mm = nc.tensor.matmul(ps[:, 6 + h // 8, (h % 8) * HD:(h % 8 + 1) * HD], pt_sb[:, i // 2, at:at + P],
                                          v2[:, n - 1 + half, (h // 8) * HD:(h // 8 + 1) * HD],
                                          start=(half == halves(n)[0]), stop=(half == 1))
            mm.then_inc(S("weighed"), 1)

        def turn_outputs(n):
            pe.wait_ge(S("o_tok_ready"), 2 * n + 2)
            pe.wait_ge(S("pt_copied"), 8 * n + 8)
            for k in range(KT):
                mm = nc.tensor.transpose(ps[:, 4 + k // 4, (k % 4) * P:(k % 4 + 1) * P],
                                         o_tok[:, k // 4, (k % 4) * P:(k % 4 + 1) * P], const("ident", P))
                if k % 4 == 3:
                    mm.then_inc(S("o_turned"), 1)

        STEPS = 4 * BLOCKS
        scores(0)
        for s in range(STEPS):
            parts = gate_parts(s)
            if parts:
                gate_part(*parts[0])
            if s and s % 4 == 0:
                turn_outputs(s // 4 - 1)
            if s + 1 < STEPS:
                scores(s + 1)
            turn_probs(s)
            if len(parts) > 1:
                gate_part(*parts[1])
            weigh(s)
        turn_outputs(BLOCKS - 1)

        pe.wait_ge(S("gate_tanh"), 16)
        pe.wait_ge(S("bT_copied"), 2 * BLOCKS)
        for m in range(KT):
            u = FIRST["out2"] + m
            wait_unit(u)
            for k in range(KT):
                if m == 0:
                    pe.wait_ge(S("y2_ready"), k + 1)
                mm = channels(ps[:, (m + 7) % 8, :], u % 2, y2_hi, y2_lo, [k])
            mm.then_inc(S("units_done"), 1)
        sum_tiles(6, x_done(2, 0))
        ffn(1, "up2", "down2", 4)

        for n in range(2 * BLOCKS):
            half, t = n // BLOCKS, n % BLOCKS
            pe.wait_ge(S("final_ready"), 4 * half + 4)
            if half == 0:
                bank = (7, 0, 1, 2)[t]
            else:
                pe.wait_ge(S("final_ready"), 8)
                bank = 3 + t
            for r in range(4):
                k = 4 * half + r
                mm = nc.tensor.transpose(ps[:, bank, r * P:(r + 1) * P], xT[:, k, t * P:(t + 1) * P], const("ident", P))
            mm.then_inc(S("result_turned"), 1)

    @block.scalar
    def _(act):
        order = Order(act, S("scalar_order"))

        def activate(*args, **kw):
            return nc.scalar.activation(*args, **kw)

        act.dma_start(cst[:, :], a["consts"]).then_inc(S("consts_loaded"), 16)
        load_par_rows(act, 0)

        def square(k, m, src, wait, n=T):
            wait(m)
            dst = norm_sq[:, m % 2, 0:n]
            if k > 2:
                if m >= 2:
                    act.wait_ge(S("square_used"), 7 * (k - 3) + m - 1)
                elif k == 3:
                    act.wait_ge(S("norm_added"), 21)
                else:
                    act.wait_ge(S("norm_ss"), k)
            elif m == 0:
                if k >= 1:
                    act.wait_ge(S("norm_ss"), k)
                dst = norm_acc[:, 0:n]
            elif m >= 3:
                act.wait_ge(S("norm_added"), 7 * k + m - 2)
            activate(dst, src(m), ACT.Square).then_inc(S("norm_squared"), 1)

        def load_sqrt(i):
            activate(small[:, 82 + i:83 + i], const("one"), ACT.Sqrt).then_inc(S("sqrt_loaded"), 1)

        def root(k, n=T):
            act.wait_ge(S("norm_ss"), k + 1)
            activate(norm_root[:, 0:n], ps[:, 7, 0:n], ACT.Sqrt, bias=const("eps"), scale=1.0 / D).then_inc(S("norm_rooted"), 1)

        def shifted(i, m, dst, shift, n=T):
            act.wait_ge(S("norm_scaled"), KT * i + m + 1)
            activate(dst[:, m, :], normed(m)[:, 0:n], ACT.Identity, bias=shift(m)).then_inc(S("h_hi_ready"), 1)
            if i == 2 and m % 2:
                act.wait_ge(S("h_hi_ready"), KT * i + m + 1)
                activate(normed(m), normed(m), ACT.Identity, bias=shift(m)).then_inc(S("shifted"), 1)

        act.wait_ge(S("turned_out"), 10)
        activate(cond[:, :, 0], column("c", 0, KT), ACT.Silu).then_inc(S("cond_ready"), 1)
        activate(cond[:, :, 1], column("c_ctx", 0, KT), ACT.Silu).then_inc(S("cond_ready"), 1)
        act.wait_ge(S("gw_cleared"), 2)
        gwv = gw[:, :].rearrange("r (h d e) -> r h d e", h=GH, d=2)
        for d, (w, b) in enumerate((("w_af", "b_af"), ("w_ab", "b_ab"))):
            act.dma_start(gwv[16 * d:16 * d + 16, :, d, :], a[w].rearrange("r (h e) -> r h e", h=GH)).then_inc(S("gw_loaded"), 16)
            act.dma_start(gwv[32:33, :, d, :], a[b].rearrange("(r h e) -> r h e", r=1, h=GH)).then_inc(S("gw_loaded"), 16)
        act.dma_start(masks[:, :, :], a["masks"]).then_inc(S("masks_loaded"), 16)
        act.dma_start(head_norms[:, 0, :], a["q_norm_2"].partition_broadcast(P)).then_inc(S("heads_loaded"), 16)
        act.dma_start(head_norms[:, 1, :], a["k_norm_2"].partition_broadcast(P)).then_inc(S("heads_loaded"), 16)
        act.dma_start(sinks[:, :], a["sinks_2"].partition_broadcast(P)).then_inc(S("heads_loaded"), 16)
        with nc.allow_non_contiguous_dma(reason="512 positions, tokens on partitions"):
            act.dma_start(positions[:, :], a["positions_2"].rearrange("(t p) -> p t", p=P)).then_inc(S("heads_loaded"), 16)
        for m in range(KT):
            square(0, m, lambda m: xT[:, m, :], lambda m: act.wait_ge(S("turned_out"), m + 1))
        root(0)
        for m in range(KT):
            square(1, m, lambda m: ctxT[:, m, :], lambda m: act.wait_ge(S("turned_out"), 10 + m // 2 + 1), TC)
        act.wait_ge(S("rinv_ready"), 1)
        root(1, TC)
        for i in range(4):
            act.wait_ge(S("ada_first_used"), 2 * i + 2)
            activate(v_tok[0:2, i, :], ps[0:2, 2 + i, :], ACT.Copy).then_inc(S("ada_rows"), 1)
        act.wait_ge(S("mod_ready"), 1)
        for m in range(KT):
            shifted(0, m, h_hi, lambda m: mod[:, m, 0:1])
        for m in range(KT):
            shifted(1, m, hc_hi, lambda m: mod[:, m, 1:2], TC)

        def copy_k(j):
            act.wait_ge(S("units_done"), FIRST["k"] + j + 1)
            bank = 2 - 2 * j
            for i in range(2):
                activate(p2[0:DK, 2 * j + i, :], ps[i * DK:(i + 1) * DK, bank, :], ACT.Copy).then_inc(S("proj_copied"), 1)
                activate(k_ctx[0:DK, 2 * j + i, :], ps[i * DK:(i + 1) * DK, bank + 1, 0:TC], ACT.Copy).then_inc(S("proj_copied"), 1)

        def gate_abs(c):
            act.wait_ge(S("gates_mm"), c + 1)
            activate(G[:, c, :], ps[:, 4 + c % 2, :], ACT.Abs).then_inc(S("gate_abs"), 1)

        act.wait_ge(S("units_done"), FIRST["low"] + 1)
        activate(al[0:32, 0:T], ps[0:32, 0, :], ACT.Copy).then_inc(S("low_copied"), 1)
        activate(al[0:32, T:T + TC], ps[0:32, 1, 0:TC], ACT.Copy).then_inc(S("low_copied"), 1)
        copy_k(0)
        for c in range(3):
            gate_abs(c)
        copy_k(1)
        for c in range(3, ALL_CHUNKS):
            gate_abs(c)

        act.wait_ge(S("gate_abs"), ALL_CHUNKS)
        for f, kw in ((ACT.Exp, {"scale": -1.0}), (ACT.Ln, {"bias": const("one")})):
            for i in range(2):
                ins = activate(G[:, 3 * i:3 * i + 3, :], G[:, 3 * i:3 * i + 3, :], f, **kw)
                if f == ACT.Exp:
                    order.done(ins)
                else:
                    ins.then_inc(S("gate_log"), 1)
            order.wait()

        def copy_sums(c):
            act.wait_ge(S("sums_mm"), c + 1)
            activate(B[:, :, c * P:(c + 1) * P], ps[:, 0, :].rearrange("p (h t) -> p h t", h=GH), ACT.Copy)\
                .then_inc(S("sums_copied"), 1)

        for j in range(2):
            act.wait_ge(S("units_done"), FIRST["q"] + j + 1)
            for i in range(2):
                activate(p1[0:DK, 2 * j + i, :], ps[i * DK:(i + 1) * DK, 6 + j, :], ACT.Copy, scale=DK ** -0.5)\
                    .then_inc(S("proj_copied"), 1)
        act.wait_ge(S("gate_done"), 2)
        for c in range(ALL_CHUNKS):
            copy_sums(c)
        act.wait_ge(S("units_done"), FIRST["v"] + 4)
        act.wait_ge(S("ada_added"), 2 * ADA_PIECES)
        for c in range(ALL_CHUNKS):
            activate(v_tok[:, c, :], ps[:, 2 + c, :], ACT.Copy).then_inc(S("v_copied"), 1)

        for n in range(ALL_CHUNKS):
            act.wait_ge(S("ke_offset"), n + 1)
            e = g_e[:, n % 2, :]
            activate(e, e, ACT.Exp, scale=-1.0 / TAU).then_inc(S("ke_decay"), 1)
            if n == ALL_CHUNKS - 1:
                activate(small[:, 0:GH * ALL_CHUNKS].rearrange("p (h c) -> p h c", h=GH), dec[:, :, :], ACT.Exp,
                         scale=1.0 / TAU).then_inc(S("decay_ready"), 1)
            act.wait_ge(S("ke_turned"), n + 1)
            if n >= 2:
                act.wait_ge(S("state_mm"), n - 1)
            activate((g_qe, g_att)[n % 2][:, :], ps[:, 4 + 3 * (n % 2), :], ACT.Copy).then_inc(S("ket_copied"), 1)

        def exp_level(step):
            if step >= LV * CHUNKS:
                return
            act.wait_ge(S("offset_ready"), step + 1)
            e = g_e[:, step % 2, :].rearrange("p (g s t) -> p g s t", s=2, t=LEVELS[step % LV])
            activate(e[:, :, 1, :], e[:, :, 1, :], ACT.Exp, scale=const("sign")).then_inc(S("e_ready"), 1)
            activate(e[:, :, 0, :], e[:, :, 0, :], ACT.Exp, scale=const("nsign")).then_inc(S("e_ready"), 1)

        def query_decay(c):
            if c == 0:
                act.wait_ge(S("state_mm"), ALL_CHUNKS)
            else:
                act.wait_ge(S("outputs_mm"), c)
            activate(g_qe[:, :].rearrange("p (h t) -> p h t", h=GH), B[:, :, c * P:(c + 1) * P], ACT.Exp,
                     scale=1.0 / TAU).then_inc(S("qe_decay"), 1)

        def branch_in(i):
            u = FIRST["branch"] + 4 * i
            act.wait_ge(S("units_done"), u + 1)
            activate(og[:, i, :], ps[:, 0, :], ACT.Tanh, scale=0.5).then_inc(S("branch_act"), 1)
            act.wait_ge(S("units_done"), u + 3)
            if i >= 1:
                act.wait_ge(S("branch_dve"), 3 * i)
            if i >= 2:
                act.wait_ge(S("o_ss"), i - 1)
            activate(c_sc[:, :], ps[:, 2, :], ACT.Copy).then_inc(S("branch_act"), 1)

        def branch_center(i):
            act.wait_ge(S("branch_dve"), 3 * i + 1)
            if i >= 1:
                act.wait_ge(S("y_ready"), i)
            activate(c_acc[:, :], c_p[:, :], ACT.Identity, scale=column("w_sc", 4 + i), bias=column("b_sc", i))\
                .then_inc(S("conv_center"), 1)

        def branch_hi(i):
            act.wait_ge(S("branch_dve"), 3 * i + 3)
            activate(ys_hi[:, i, :], c_acc[:, :], ACT.Copy).then_inc(S("y_hi_ready"), 1)

        def copy_output(c):
            act.wait_ge(S("outputs_mm"), c + 1)
            activate(oT[:, :, c * P:(c + 1) * P], ps[:, 6, :].rearrange("p (h t) -> p h t", h=GH), ACT.Copy)\
                .then_inc(S("o_copied"), 1)

        def head_square(c):
            act.wait_ge(S("o_copied"), c + 1)
            act.wait_ge(S("branch_dve"), 3 * min(c + 1, CHUNKS - 1) + 1)
            if c == CHUNKS - 1:
                act.wait_ge(S("o_ss"), c)
            activate(c_sc[:, :].rearrange("p (h t) -> p h t", h=GH), oT[:, :, c * P:(c + 1) * P], ACT.Square)\
                .then_inc(S("o_squared"), 1)

        def head_root(c):
            act.wait_ge(S("o_ss"), c + 1)
            act.wait_ge(S("branch_dve"), 3 * min(c + 1, CHUNKS - 1) + 3)
            if c == CHUNKS - 1:
                act.wait_ge(S("head_scaled"), c)
            activate(c_p[:, :], ps[:, 6, :], ACT.Sqrt, bias=const("eps4"), scale=4.0 / DV).then_inc(S("o_rooted"), 1)

        exp_level(0)
        exp_level(1)
        for c in range(CHUNKS):
            for n in range(LV):
                exp_level(LV * c + n + 2)
                if n == 0:
                    branch_in(c)
                    if c >= 1:
                        copy_output(c - 1)
                    branch_center(c)
                elif n == 1:
                    branch_hi(c)
                    if c >= 1:
                        head_square(c - 1)
                elif n == 2:
                    query_decay(c)
                elif n == 3 and c >= 1:
                    head_root(c - 1)
        copy_output(CHUNKS - 1)
        head_square(CHUNKS - 1)
        head_root(CHUNKS - 1)
        for h in range(GH):
            act.wait_ge(S("head_gated"), 2)
            activate(yg_hi[:, h, :], oT[:, h, :], ACT.Copy).then_inc(S("y_hi_ready"), 1)

        def post_squares(k, wait, first_tile):
            for m in range(KT):
                square(k, m, lambda m: ps[:, (m + 7) % 8, :], wait)
                if m == 0:
                    activate(first_tile, ps[:, 7, :], ACT.Copy).then_inc(S("mo_copied"), 1)
            act.wait_ge(S("rinv_ready"), k)
            root(k)

        act.wait_ge(S("y_ready"), 8)
        post_squares(2, lambda m: act.wait_ge(*out_ready(m)), mo[:, 0, :])

        def modulate(k, i, shift, residual):
            for m in range(KT):
                square(k, m, lambda m: xT[:, m, :], lambda m: act.wait_ge(*x_done(residual, m)))
            act.wait_ge(S("rinv_ready"), k)
            root(k)
            for m in range(KT):
                shifted(i, m, h_hi, shift)

        modulate(3, 2, lambda m: mod[:, 24 + m, 0:1], 0)

        def ffn_pair(i, up, j, s, n):
            u = FIRST[up]
            act.wait_ge(S("units_done"), j * 2 + (u + 1))
            act.wait_ge(S("f_hi_ready"), n + 1)
            activate(f_acc[:, s, :], ps[:, 2 * s, :], ACT.Identity,
                     scale=column("w_cf_a", j + 4 * FT) if i == 0 else column("conv_w_2_b", j),
                     bias=column("b_cf" if i == 0 else "conv_b_2", j)).then_inc(S("centered"), 1)
            if i == 1:
                act.wait_ge(S("f_ready"), n + 1)
                act.wait_ge(S("units_done"), j * 2 + (u + 2))
                activate(f_act[:, s, :], ps[:, 2 * s + 1, :], ACT.Identity, scale=column("conv_w_2_b", j + FT),
                         bias=column("conv_b_2", j + FT)).then_inc(S("centered_val"), 1)
            act.wait_ge(S("taps_done"), n + 1)
            if i == 0:
                act.wait_ge(S("f_ready"), n + 1)
            activate((f_act if i == 0 else f_acc)[:, s, :], f_acc[:, s, :], ACT.Silu).then_inc(S("silu_done"), 1)
            act.wait_ge(S("gated"), n + 1)
            activate(f_hi[:, bass.ds(j, 1), :].rearrange("p a t -> p (a t)"), f_act[:, s, :], ACT.Copy).then_inc(S("f_hi_ready"), 1)

        def ffn(i, up):
            with act.Fori(0, FT // 2) as turn:
                activate(small[:, 84 + i:85 + i], const("one"), ACT.Silu).then_inc(S("silu_loaded"), 1)
                for s in range(2):
                    ffn_pair(i, up, turn * 2 + s, s, turn * 2 + (s + FT * i))

        ffn(0, "up")

        def down_wait(i, down):
            return lambda m: act.wait_ge(S("down_done"), 7 * i + m + 1) if m < KT - 1 else \
                act.wait_ge(S("units_done"), FIRST[down] + FT)

        load_sqrt(0)
        post_squares(4, down_wait(0, "down"), mo2[:, :])
        modulate(5, 3, lambda m: const("zero"), 1)

        for n, (name, cols) in enumerate((("q2a", slice(0, 512)), ("q2b", slice(512, 1024)))):
            act.wait_ge(S("units_done"), FIRST[name] + 4)
            for t in range(BLOCKS):
                activate(qkv[:, t, cols], ps[:, 4 * n + t, :], ACT.Copy).then_inc(S("qkv_copied"), 1)
        act.wait_ge(S("units_done"), FIRST["kv2"] + 2)
        for t in range(BLOCKS):
            activate(qkv[:, t, 1024:1152], ps[:, t, 0:P], ACT.Copy).then_inc(S("qkv_copied"), 1)
            activate(v2[:, t, :], ps[:, t, P:2 * P], ACT.Copy).then_inc(S("qkv_copied"), 1)

        act.wait_ge(S("angles_ready"), 1)
        activate(trig[:, 4, :], trig[:, 2, :], ACT.Sin).then_inc(S("sines_ready"), 1)
        activate(trig[:, 5, :], trig[:, 3, :], ACT.Sin, scale=-1.0, bias=const("half_pi")).then_inc(S("sines_ready"), 1)
        act.wait_ge(S("qkv_copied"), 16)
        for t in range(BLOCKS):
            activate(squares2[:, t, :], qkv[:, t, :], ACT.Square).then_inc(S("qk_squared"), 1)

        def pool_copy(p):
            act.wait_ge(S("units_done"), pool_unit(p) + 1)
            if p >= 2:
                act.wait_ge(S("pooled"), p - 1)
            activate(pw[:, p % 2, :], ps[:, 4 + p % 4, :], ACT.Copy).then_inc(S("pool_copied"), 1)

        def pool_hi(p):
            act.wait_ge(S("pooled"), p + 1)
            g = p // 2
            activate(pl_hi[:, p, :], pw[:, 2 + (g + 1) % 2, :], ACT.Copy).then_inc(S("pl_hi_ready"), 1)

        act.wait_ge(S("qk_summed"), 1)
        activate(small[:, 0:72], small[:, 0:72], ACT.Sqrt, bias=const("eps"), scale=1.0 / HD).then_inc(S("qk_rooted"), 1)
        act.wait_ge(S("qk_ready"), 1)
        pool_copy(0)
        pool_copy(1)

        def gate(s):
            act.wait_ge(S("units_done"), gate_unit(s) + 1)
            if s >= 8:
                act.wait_ge(S("pool_gated"), s - 7)
            activate(ga[:, s % 8, :], ps[:, s % 2, :], ACT.Tanh, scale=0.5, bias=half_gate_bias[:, s:s + 1]).then_inc(S("gate_tanh"), 1)

        def turned(n):
            act.wait_ge(S("q_turned"), n + 1)
            if n < 8:
                activate(qT[:, 4 * (n % 2):4 * (n % 2) + 4, (n // 2) * P:(n // 2 + 1) * P],
                         ps[:, 2 + n % 2, :].rearrange("p (k t) -> p k t", k=4), ACT.Copy).then_inc(S("qT_copied"), 1)
            else:
                activate(kT[:, n - 8, :], ps[:, 2 + n % 2, :], ACT.Copy).then_inc(S("qT_copied"), 1)

        def turned_and_gates(i):
            turned(2 * i)
            turned(2 * i + 1)
            for s in (0, 1) if i == 0 else (i + 1,):
                gate(s)

        for p in range(8):
            pool_hi(p)
            if p + 2 < 8:
                pool_copy(p + 2)
            if p >= 5:
                turned_and_gates(p - 5)
        turned_and_gates(3)
        turned_and_gates(4)

        STEPS = 4 * BLOCKS

        def stat(s, i):
            n = (s // 4) % 2
            h = 4 * (s % 4)
            return att_stat[:, n, i, h:h + 4]

        def probs(s):
            n = s // 4
            act.wait_ge(S("max_negated"), s + 1)
            keys = slice(0 if n else P, 2 * P)
            for i in range(4):
                t = scores_sb[:, (s % 2) * 4 + i, keys]
                activate(t, t, ACT.Exp, bias=stat(s, 1)[:, i:i + 1], accum_out=stat(s, 2)[:, i:i + 1]).then_inc(S("probs_ready"), 1)
            if s % 4 == 3:
                act.wait_ge(S("sink_offset"), n + 1)
                activate(att_stat[:, n % 2, 3, :], att_stat[:, n % 2, 3, :], ACT.Exp).then_inc(S("sink_part"), 1)

        def copy_probs(s):
            n = s // 4
            if s >= 1:
                act.wait_ge(S("weighed"), s)
            for i in range(2):
                act.wait_ge(S("probs_turned"), 2 * s + i + 1)
                v = lambda t: t.rearrange("p (h c t) -> p h c t", h=2, c=2)[:, :, (0 if n else 1):, :]
                activate(v(pt_sb[:, i, :]), v(ps[:, 4 + i, :]), ACT.Copy).then_inc(S("pt_copied"), 1)

        def copy_outputs(n):
            for i in range(2):
                act.wait_ge(S("o_turned"), 2 * n + i + 1)
                activate(qT[:, 4 * i:4 * i + 4, n * P:(n + 1) * P], ps[:, 4 + i, :].rearrange("p (k t) -> p k t", k=4), ACT.Copy)\
                    .then_inc(S("bT_copied"), 1)

        for s in range(STEPS):
            probs(s)
            if s and gate_done_in(s - 1):
                gate(gate_done_in(s - 1))
            if s and s % 4 == 0:
                copy_outputs(s // 4 - 1)
            copy_probs(s)
        copy_outputs(BLOCKS - 1)
        for k in range(KT):
            if k % 4 == 0:
                act.wait_ge(S("y2_sum"), k // 4 + 1)
            activate(y2_hi[:, k, :], qT[:, k, :], ACT.Copy).then_inc(S("y2_hi_ready"), 1)

        load_sqrt(1)
        modulate(6, 4, lambda m: const("zero"), 2)
        ffn(1, "up2")
        for n in range(2 * BLOCKS):
            half, t = n // BLOCKS, n % BLOCKS
            act.wait_ge(S("result_turned"), n + 1)
            bank = (7, 0, 1, 2)[t] if half == 0 else 3 + t
            activate(result[:, t, 512 * half:512 * half + 512], ps[:, bank, :], ACT.Copy).then_inc(S("result_copied"), 1)

    @block.vector
    def _(dve):
        order = Order(dve, S("vector_order"))
        vec = nc.vector

        vec.memset(par_rows[:, :, :], 0.0).then_inc(S("rows_cleared"), 1)
        vec.memset(small[:, 80:81], 0.0).then_inc(S("f_hi_ready"), 2)
        vec.memset(small[:, 81:82], 0.0).then_inc(S("f_ready"), 2)
        for n in range(14):
            dve.wait_ge(S("turned"), n + 1)
            if n < 8:
                dst, src = xT[:, n, :], ps[:, n % 6, :]
            elif n < 10:
                dst, src = par[:, 3 * (n - 8) * P:3 * (n - 7) * P], ps[:, n % 6, 0:3 * P]
            else:
                dst, src = ctxT[:, 2 * (n - 10):2 * (n - 10) + 2, :].rearrange("p k t -> p (k t)"), ps[:, n % 6, :]
            vec.tensor_copy(dst, src).then_inc(S("turned_out"), 1)
            if n == 9:
                vec.memset(gw[:, :], 0.0).then_inc(S("gw_cleared"), 1)
                vec.memset(al[32:33, :], 1.0).then_inc(S("gw_cleared"), 1)

        def add_squares(k, n=T):
            for m in range(1, KT):
                dve.wait_ge(S("norm_squared"), KT * k + m + 1)
                if m >= 2:
                    dve.wait_ge(S("norm_added"), 7 * k + m - 1)
                vec.tensor_tensor(norm_acc[:, 0:n], norm_acc[:, 0:n], norm_sq[:, m % 2, 0:n], ALU.add)\
                    .then_inc(S("norm_added"), 1)

        def invert(k, n=T, rinv=norm_rinv):
            dve.wait_ge(S("norm_rooted"), k + 1)
            vec.reciprocal(rinv[:, 0:n], norm_root[:, 0:n]).then_inc(S("rinv_ready"), 1)

        def scaled(i, m, src, scale, n=T, rinv=norm_rinv):
            if m >= 4:
                dve.wait_ge(*h_done(i, m - 4))
            elif i == 1:
                dve.wait_ge(*h_done(0, m + 4))
            vec.scalar_tensor_tensor(normed(m)[:, 0:n], src(m), scale(m), rinv[:, 0:n], ALU.mult, ALU.mult)\
                .then_inc(S("norm_scaled"), 1)

        def low_part(i, m, hi, lo, shift, n=T):
            if i >= 2 and m % 2:
                return
            dve.wait_ge(S("h_hi_ready"), KT * i + m + 1)
            vec.scalar_tensor_tensor(lo[:, m, :], normed(m)[:, 0:n], shift(m), hi[:, m, :].bitcast(F32),
                                     ALU.add, ALU.subtract).then_inc(S("h_ready"), 1)

        def modulated(k, i, src, scale, shift, hi, lo, n=T, rinv=norm_rinv):
            dve.wait_ge(S("rinv_ready"), k + 1)
            for m in range(KT):
                scaled(i, m, src, scale, n, rinv)
                if m >= 1:
                    low_part(i, m - 1, hi, lo, shift, n)
            low_part(i, KT - 1, hi, lo, shift, n)

        add_squares(0)
        invert(0)
        add_squares(1, TC)
        invert(1, TC, rinv_ctx)
        dve.wait_ge(S("ada_turned"), 1)
        order.done(vec.tensor_tensor(mod[:, 0:16, :], ps[:, 6, 0:32].rearrange("p (m i) -> p m i", i=2),
                                     column("b_ada", 0, 16).unsqueeze(2).broadcast_to([P, 16, 2]), ALU.add))
        order.wait()
        for i in range(2):
            ins = vec.scalar_tensor_tensor(scale_in[:, i, :], mod[:, 8:16, i], 1.0, column("g_pre_mix", 0, KT), ALU.add, ALU.mult)
            if i == 0:
                order.done(ins)
        ins.then_inc(S("mod_ready"), 1)
        dve.wait_ge(S("mod_ready"), 1)
        modulated(0, 0, lambda m: xT[:, m, :], lambda m: scale_in[:, 0, m:m + 1], lambda m: mod[:, m, 0:1], h_hi, h_lo)
        modulated(1, 1, lambda m: ctxT[:, m, :], lambda m: scale_in[:, 1, m:m + 1], lambda m: mod[:, m, 1:2], hc_hi, hc_lo, TC,
                  rinv_ctx)

        gate_min = B[:, :, :].rearrange("p h t -> p (h t)").rearrange("p (c n) -> p c n", c=ALL_CHUNKS)
        def ada_piece(n):
            dve.wait_ge(ada_loaded[n % PIECE_SLOTS], 16 * (n // PIECE_SLOTS + 1))
            chunk = n // 4
            acc = ada_acc[chunk % 2][:, :]
            if n % 4 == 0 and chunk >= 2:
                dve.wait_ge(S("ada_out"), chunk - 1)
            for kk in range(2):
                k = 2 * (n % 4) + kk
                w, s = ada_slot(n)[:, kk, :], cond[:, k, 0:1]
                if k == 0:
                    ins = vec.tensor_scalar(acc, w, s, None, ALU.mult)
                else:
                    dve.wait_ge(S("ada_added"), 2 * n + kk)
                    ins = vec.scalar_tensor_tensor(acc, w, s, acc, ALU.mult, ALU.add)
                ins.then_inc(S("ada_added"), 1)

        def late_modulation():
            dve.wait_ge(S("ada_out"), 8)
            order.done(vec.tensor_tensor(mod[:, 16:48, 0], ps[:, 1, 0:32], column("b_ada", 16, 32), ALU.add))
            order.wait()
            order.done(vec.tensor_tensor(gate_out[:, 0, :], mod[:, 16:24, 0], column("g_post_mix", 0, KT), ALU.mult))
            order.done(vec.tensor_tensor(gate_out[:, 1, :], mod[:, 40:48, 0], column("g_post_ffn", 0, KT), ALU.mult))
            vec.scalar_tensor_tensor(scale_in[:, 2, :], mod[:, 32:40, 0], 1.0, column("g_pre_ffn", 0, KT), ALU.add, ALU.mult)\
                .then_inc(S("mod_ready"), 1)

        for c in range(ALL_CHUNKS):
            dve.wait_ge(S("gate_abs"), c + 1)
            vec.tensor_scalar(gate_min[:, c, :], ps[:, 4 + c % 2, :], 0.0, None, ALU.min).then_inc(S("gate_min"), 1)
            ada_piece(c)
        dve.wait_ge(S("proj_copied"), 8)
        vec.tensor_copy(p1[DK:P, :, :], p2[0:DK, :, :]).then_inc(S("p_copied"), 1)
        vec.tensor_copy(k_ctx[DK:P, :, :], k_ctx[0:DK, :, :]).then_inc(S("p_copied"), 1)
        for n in range(6, 10):
            ada_piece(n)
        dve.wait_ge(S("gate_min"), ALL_CHUNKS)
        for i in range(2):
            dve.wait_ge(S("gate_log"), i + 1)
            cs = slice(3 * i, 3 * i + 3)
            vec.tensor_tensor(G[:, cs, :], gate_min[:, cs, :], G[:, cs, :], ALU.subtract).then_inc(S("gate_done"), 1)
        dve.wait_ge(S("proj_copied"), 12)
        vec.tensor_copy(p2[DK:P, :, :], p1[0:DK, :, :]).then_inc(S("p_copied"), 1)
        for n in range(10, ADA_PIECES):
            ada_piece(n)

        dve.wait_ge(S("sums_copied"), ALL_CHUNKS)
        Bc = B[:, :, :].rearrange("p h (c t) -> p h c t", t=P)
        order.done(vec.tensor_copy(dec[0:DK, :, :], Bc[0:DK, :, :, P - 1]))
        order.done(vec.tensor_copy(dec[DK:P, :, :], Bc[DK:P, :, :, 0]))
        order.wait()
        dve.wait_ge(S("p_copied"), 3)

        def ke_offset(n, c):
            if n >= 2:
                dve.wait_ge(S("ke_ready"), n - 1)
            vec.tensor_tensor(g_e[:, n % 2, :].rearrange("p (h t) -> p h t", h=GH), Bc[:, :, c, :],
                              dec[:, :, c:c + 1].broadcast_to([P, GH, P]), ALU.subtract).then_inc(S("ke_offset"), 1)

        def ke(n, c):
            dve.wait_ge(S("ke_decay"), n + 1)
            if n >= 2:
                dve.wait_ge(S("ke_turned"), n - 1)
            e, z = (b[:, n % 2, :].rearrange("p (h t) -> p h t", h=GH) for b in (g_e, g_z))
            if c >= CHUNKS:
                ins = vec.tensor_tensor(z, e, k_ctx[:, :, (c - CHUNKS) * P:(c - CHUNKS + 1) * P], ALU.mult)
            else:
                vec.tensor_tensor(z[0:DK], e[0:DK], p2[0:DK, :, c * P:(c + 1) * P], ALU.mult)
                ins = vec.tensor_tensor(z[DK:P], e[DK:P], p1[DK:P, :, c * P:(c + 1) * P], ALU.mult)
            ins.then_inc(S("ke_ready"), 1)

        def keep_state(n, c):
            dve.wait_ge(S("state_mm"), n + 1)
            fwd = {4: s_tmp[0:DK, :], 5: SS[0:DK, 0, :], 0: SS[0:DK, 1, :], 1: SS[0:DK, 2, :], 2: SS[0:DK, 3, :]}
            bwd = {5: s_tmp[DK:P, :], 4: SS[DK:P, 3, :], 3: SS[DK:P, 2, :], 2: SS[DK:P, 1, :], 1: SS[DK:P, 0, :]}
            todo = ([(fwd[c], ps[0:DK, 5, :])] if c in fwd else []) + ([(bwd[c], ps[DK:P, 5, :])] if c in bwd else [])
            for dst, src in todo:
                ins = vec.tensor_copy(dst, src)
            ins.then_inc(S("state_read"), 1)

        ke_offset(0, STATE_ORDER[0])
        late_modulation()
        for n, c in enumerate(STATE_ORDER):
            if n + 1 < ALL_CHUNKS:
                ke_offset(n + 1, STATE_ORDER[n + 1])
            ke(n, c)
            if n >= 1:
                keep_state(n - 1, STATE_ORDER[n - 1])
        keep_state(ALL_CHUNKS - 1, STATE_ORDER[-1])
        def view(t, c, n):
            return t[:, :, c * P:(c + 1) * P].rearrange("p h (b s t) -> p h b s t", s=2, t=LEVELS[n])

        def flat(t, n):
            return t.rearrange("p (h b s t) -> p h b s t", h=GH, s=2, t=LEVELS[n])

        def offset(step):
            if step >= LV * CHUNKS:
                return
            c, n = step // LV, step % LV
            half = LEVELS[n]
            if step >= 2:
                dve.wait_ge(S("z_ready"), 2 * step - 2)
            b = B[:, :, c * P:(c + 1) * P].rearrange("p h (b t) -> p h b t", t=2 * half)
            vec.tensor_tensor(g_e[:, step % 2, :].rearrange("p (h b t) -> p h b t", h=GH, t=2 * half), b,
                              b[:, :, :, half:half + 1].broadcast_to([P, GH, P // (2 * half), 2 * half]),
                              ALU.subtract).then_inc(S("offset_ready"), 1)

        def decayed(step):
            c, n = step // LV, step % LV
            dve.wait_ge(S("e_ready"), 2 * step + 2)
            for side, src in ((1, p1), (0, p2)):
                vec.tensor_tensor(flat(g_z[:, step % 2, :], n)[:, :, :, side, :], flat(g_e[:, step % 2, :], n)[:, :, :, side, :],
                                  view(src, c, n)[:, :, :, side, :], ALU.mult).then_inc(S("z_ready"), 1)

        def take(step):
            c, n = step // LV, step % LV
            dve.wait_ge(S("level_mm"), step + 1)
            if n:
                dve.wait_ge(S("att_taken"), taken(step - 1))
            elif c:
                dve.wait_ge(S("outputs_mm"), c)
            half = LEVELS[n]
            for bank, side in ((4, 1), (5, 0)):
                dst = flat(g_att[:, :], n)[:, :, :, side, :]
                src = ps[:, bank, 0:256].rearrange("p (h b t) -> p h b t", h=GH, t=half)
                if n == 0:
                    ins = vec.tensor_copy(dst, src)
                else:
                    m = masks[:, n - 1, :].rearrange("p (b s t) -> p b s t", s=2, t=half)[:, :, side, :]
                    ins = vec.copy_predicated(dst, m.unsqueeze(1).broadcast_to([P, GH, P // (2 * half), half]), src)
                ins.then_inc(S("att_taken"), 1)
            if n == LV - 1:
                dve.wait_ge(S("diag_mm"), c + 1)
                dve.wait_ge(S("att_taken"), taken(step) - 1)
                vec.copy_predicated(g_att[:, :].rearrange("p (h t) -> p h t", h=GH),
                                    masks[:, 6, :].unsqueeze(1).broadcast_to([P, GH, P]),
                                    ps[:, 6, :].rearrange("p (h t) -> p h t", h=GH)).then_inc(S("att_taken"), 1)

        def query_decayed(c):
            dve.wait_ge(S("qe_decay"), c + 1)
            q = g_qe[:, :].rearrange("p (h t) -> p h t", h=GH)
            vec.tensor_tensor(q[0:DK], q[0:DK], p1[0:DK, :, c * P:(c + 1) * P], ALU.mult).then_inc(S("qe_ready"), 1)
            vec.tensor_tensor(q[DK:P], q[DK:P], p2[DK:P, :, c * P:(c + 1) * P], ALU.mult).then_inc(S("qe_ready"), 1)

        def branch_product(i):
            dve.wait_ge(S("branch_act"), 2 * i + 2)
            dve.wait_ge(S("units_done"), FIRST["branch"] + 4 * i + 4)
            if i >= 2:
                dve.wait_ge(S("head_scaled"), i - 1)
            vec.tensor_tensor(c_p[:, :], c_sc[:, :], ps[:, 3, :], ALU.mult).then_inc(S("branch_dve"), 1)
            vec.scalar_tensor_tensor(og[:, i, :], og[:, i, :], 1.0, ps[:, 0, :], ALU.add, ALU.mult).then_inc(S("branch_dve"), 1)

        def branch_taps(i):
            dve.wait_ge(S("conv_center"), i + 1)
            acc, p = (t[:, :].rearrange("p (r c) -> p r c", c=GRID) for t in (c_acc, c_p))
            for tap, dst, src in ((0, acc[:, :, 1:], p[:, :, :-1]), (2, acc[:, :, :-1], p[:, :, 1:])):
                order.done(vec.scalar_tensor_tensor(dst, src, column("w_sc", 4 * tap + i), dst, ALU.mult, ALU.add))
                order.wait()
            vec.tensor_tensor(c_acc[:, :], c_acc[:, :], ps[:, 1, :], ALU.mult).then_inc(S("branch_dve"), 1)

        def branch_lo(i):
            dve.wait_ge(S("y_hi_ready"), i + 1)
            vec.tensor_tensor(ys_lo[:, i, :], c_acc[:, :], ys_hi[:, i, :].bitcast(F32), ALU.subtract).then_inc(S("y_ready"), 1)

        def head_scale(c):
            dve.wait_ge(S("o_rooted"), c + 1)
            order.done(vec.reciprocal(c_p[:, :], c_p[:, :]))
            order.wait()
            o = oT[:, :, c * P:(c + 1) * P]
            vec.scalar_tensor_tensor(o, o, column("g_head"), c_p[:, :].rearrange("p (h t) -> p h t", h=GH), ALU.mult, ALU.mult)\
                .then_inc(S("head_scaled"), 1)

        def head_gate(last):
            tok = slice(T - P, T) if last else slice(0, T - P)
            dve.wait_ge(S("head_scaled"), CHUNKS if last else CHUNKS - 1)
            if not last:
                dve.wait_ge(S("branch_dve"), 3 * CHUNKS)
            vec.tensor_tensor(oT[:, :, tok], oT[:, :, tok], og[:, :, tok], ALU.mult).then_inc(S("head_gated"), 1)

        dve.wait_ge(S("state_read"), ALL_CHUNKS)
        offset(0)
        offset(1)
        decayed(0)
        dve.wait_ge(S("decay_ready"), 1)

        def advance(rows, dst, src, c):
            for h in range(GH):
                cols = slice(h * P, (h + 1) * P)
                yield vec.scalar_tensor_tensor(dst[rows, cols], src[rows, cols],
                                               small[rows, h * ALL_CHUNKS + c:h * ALL_CHUNKS + c + 1],
                                               dst[rows, cols], ALU.mult, ALU.add)

        up, down = slice(0, DK), slice(DK, P)
        def advance_states(n):
            steps = list(advance(up, SS[:, n, :], s_tmp if n == 0 else SS[:, n - 1, :], CHUNKS + 1 if n == 0 else n - 1))
            m = CHUNKS - 1 - n
            steps += advance(down, SS[:, m, :], s_tmp if n == 0 else SS[:, m + 1, :], CHUNKS if n == 0 else m + 1)
            steps[-1].then_inc(S("states_done"), 1)

        dve.wait_ge(S("masks_loaded"), 16)
        for c in range(CHUNKS):
            for n in range(LV):
                step = LV * c + n
                if step:
                    decayed(step)
                offset(step + 2)
                if step >= 1:
                    take(step - 1)
                if n == 0:
                    branch_product(c)
                elif n == 1:
                    branch_taps(c)
                elif n == 2:
                    branch_lo(c)
                elif n == 3:
                    query_decayed(c)
                if c == 0 and 2 <= n < 2 + CHUNKS:
                    if n > 2:
                        dve.wait_ge(S("states_done"), n - 2)
                    advance_states(n - 2)
                if n == 4 and c >= 1:
                    head_scale(c - 1)
                elif n == 5 and c == CHUNKS - 1:
                    head_gate(False)
        take(LV * CHUNKS - 1)
        head_scale(CHUNKS - 1)
        head_gate(True)
        for h in range(GH):
            dve.wait_ge(S("y_hi_ready"), 5 + h)
            vec.tensor_tensor(yg_lo[:, h, :], oT[:, h, :], yg_hi[:, h, :].bitcast(F32), ALU.subtract).then_inc(S("y_ready"), 1)

        def gated_residual(k, r, gate, mo_tile, hs):
            invert(k)
            dve.wait_ge(S("rinv_ready"), k + 1)
            dve.wait_ge(*h_done(hs, KT - 2))
            dve.wait_ge(*h_done(hs, KT - 1))
            for m in range(KT + 1):
                if m < KT:
                    if m >= 2:
                        dve.wait_ge(*x_done(r, m - 2))
                    src = mo_tile if m == 0 else ps[:, m - 1, :]
                    vec.scalar_tensor_tensor(norm_t[:, m % 2, :], src, gate_out[:, gate, m:m + 1], norm_rinv[:, :],
                                             ALU.mult, ALU.mult).then_inc(S("branch_normed"), 1)
                if m % 2:
                    dve.wait_ge(S("branch_normed"), KT * r + m)
                    vec.tensor_tensor(xT[:, m - 1, :], xT[:, m - 1, :], norm_t[:, (m - 1) % 2, :], ALU.add)\
                        .then_inc(S("x_ready"), 1)

        dve.wait_ge(S("mod_ready"), 2)
        add_squares(2)
        dve.wait_ge(S("mo_copied"), 1)
        gated_residual(2, 0, 0, mo[:, 0, :], 1)
        invert(3)
        modulated(3, 2, lambda m: xT[:, m, :], lambda m: scale_in[:, 2, m:m + 1], lambda m: mod[:, 24 + m, 0:1], h_hi, h_lo)

        def ffn_pair(i, up, j, s, n):
            acc = f_acc[:, s, :]
            dve.wait_ge(S("centered"), n + 1)
            if i == 0:
                u = ps[:, 2 * s, :].rearrange("p (r c) -> p r c", c=GRID)
                a2 = acc.rearrange("p (r c) -> p r c", c=GRID)
                taps = [(dr, dc) for dr in range(3) for dc in range(3) if (dr, dc) != (1, 1)]
                for dr, dc in taps:
                    cut = lambda d, n: (slice(max(0, 1 - d), n - max(0, d - 1)), slice(max(0, d - 1), n - max(0, 1 - d)))
                    (ro, ri), (co, ci) = cut(dr, ROWS), cut(dc, GRID)
                    tap = 3 * dr + dc
                    w = column("w_cf_a", j + tap * FT) if tap < 5 else column("w_cf_b", j + (tap - 5) * FT)
                    ins = vec.scalar_tensor_tensor(a2[:, ro, co], u[:, ri, ci], w, a2[:, ro, co], ALU.mult, ALU.add)
                    if (dr, dc) != taps[-1]:
                        order.done(ins)
                        order.wait()
                ins.then_inc(S("taps_done"), 1)
            else:
                for bank, dst, first, sem in ((2 * s, acc, 0, "taps_done"), (2 * s + 1, f_act[:, s, :], FT, None)):
                    if first:
                        dve.wait_ge(S("centered_val"), n + 1 - FT)
                    for tap, d in ((1, 1), (0, 2)):
                        ins = vec.scalar_tensor_tensor(dst[:, d:], ps[:, bank, 0:T - d], column("conv_w_2_a", j + (tap * 2 * FT + first)),
                                                       dst[:, d:], ALU.mult, ALU.add)
                        if tap == 0 and sem:
                            ins.then_inc(S(sem), 1)
                        else:
                            order.done(ins)
                            order.wait()
            dve.wait_ge(S("silu_done"), n + 1)
            dve.wait_ge(S("units_done"), j * 2 + (FIRST[up] + 2))
            other = ps[:, 2 * s + 1, :] if i == 0 else acc
            vec.tensor_tensor(f_act[:, s, :], f_act[:, s, :], other, ALU.mult).then_inc(S("gated"), 1)
            dve.wait_ge(S("f_hi_ready"), n + 3)
            vec.tensor_tensor(f_lo[:, bass.ds(j, 1), :].rearrange("p a t -> p (a t)"), f_act[:, s, :],
                              f_hi[:, bass.ds(j, 1), :].rearrange("p a t -> p (a t)").bitcast(F32), ALU.subtract)\
                .then_inc(S("f_ready"), 1)

        def ffn(i, up):
            with dve.Fori(0, FT // 2) as turn:
                order.start(turn, 2 * (7 if i == 0 else 3), FT // 2)
                for s in range(2):
                    ffn_pair(i, up, turn * 2 + s, s, turn * 2 + (s + FT * i))
                order.end()

        ffn(0, "up")
        dve.wait_ge(S("mo_copied"), 2)
        gated_residual(4, 1, 1, mo2[:, :], 2)
        invert(5)
        modulated(5, 3, lambda m: xT[:, m, :], lambda m: column("attn_norm_2", m), lambda m: const("zero"), h_hi, h_lo)

        dve.wait_ge(S("heads_loaded"), 64)
        t4 = lambda i: trig[:, i, :].rearrange("p (t f) -> p t f", f=HALF_ROPE)

        def link(ins):
            order.done(ins)
            order.wait()

        link(vec.tensor_copy(trig[:, 0, 0:BLOCKS], positions[:, :]))
        link(vec.tensor_tensor(t4(1), trig[:, 0, 0:BLOCKS].unsqueeze(2).broadcast_to([P, BLOCKS, HALF_ROPE]),
                               const("inv_freq", HALF_ROPE).unsqueeze(1).broadcast_to([P, BLOCKS, HALF_ROPE]), ALU.mult))
        magic = 1.5 * 2.0 ** 23
        link(vec.tensor_scalar(trig[:, 0, :], trig[:, 1, :], float(np.float32(1 / (2 * np.pi))), None, ALU.mult))
        link(vec.tensor_scalar(trig[:, 0, :], trig[:, 0, :], magic, None, ALU.add))
        link(vec.tensor_scalar(trig[:, 0, :], trig[:, 0, :], magic, None, ALU.subtract))
        for part in two_pi_parts():
            link(vec.scalar_tensor_tensor(trig[:, 1, :], trig[:, 0, :], -part, trig[:, 1, :], ALU.mult, ALU.add))
        below_pi = float(np.nextafter(np.float32(np.pi), np.float32(0)))
        link(vec.tensor_scalar(trig[:, 2, :], trig[:, 1, :], below_pi, -below_pi, ALU.min, ALU.max))
        link(vec.tensor_scalar(trig[:, 3, :], trig[:, 2, :], -1.0, None, ALU.mult))
        vec.tensor_tensor(trig[:, 3, :], trig[:, 3, :], trig[:, 2, :], ALU.max).then_inc(S("angles_ready"), 1)
        link(vec.tensor_scalar(head_norms[:, 0, :], head_norms[:, 0, :], HD ** -0.5, None, ALU.mult))
        link(vec.tensor_scalar(half_gate_bias[:, :], column("b_gate_2", 0, 16), 0.5, None, ALU.mult))

        heads = lambda t: t.rearrange("p t (h e) -> p t h e", e=HD)
        dve.wait_ge(S("qk_squared"), BLOCKS)
        vec.tensor_reduce(small[:, 0:72], squares2[:, :, :].rearrange("p t (h e) -> p (t h) e", e=HD), AX.X, ALU.add)\
            .then_inc(S("qk_summed"), 1)
        dve.wait_ge(S("qk_rooted"), 1)
        link(vec.reciprocal(small[:, 0:72], small[:, 0:72]))
        q3 = qkv[:, :, :].rearrange("p t (h e) -> p (t h) e", e=HD)
        link(vec.tensor_tensor(q3, q3, small[:, 0:72].unsqueeze(2).broadcast_to([P, 72, HD]), ALU.mult))
        for i, hs in ((0, slice(0, QH)), (1, slice(QH, NQK))):
            v = heads(qkv[:, :, :])[:, :, hs, :]
            w = head_norms[:, i:i + 1, :].unsqueeze(1).broadcast_to([P, BLOCKS, hs.stop - hs.start, HD])
            link(vec.tensor_tensor(v, v, w, ALU.mult))
        x1, x2 = (heads(qkv[:, :, :])[:, :, :, i * HALF_ROPE:(i + 1) * HALF_ROPE] for i in range(2))
        r1, r2 = (rot[:, i, :].rearrange("p (t h f) -> p t h f", t=BLOCKS, f=HALF_ROPE) for i in range(2))
        sin, cos = (t4(4 + i).unsqueeze(2).broadcast_to([P, BLOCKS, NQK, HALF_ROPE]) for i in range(2))
        dve.wait_ge(S("sines_ready"), 2)
        link(vec.tensor_tensor(r1, x1, sin, ALU.mult))
        link(vec.tensor_tensor(r2, x2, sin, ALU.mult))
        link(vec.tensor_tensor(x1, x1, cos, ALU.mult))
        link(vec.tensor_tensor(x2, x2, cos, ALU.mult))
        link(vec.tensor_tensor(x1, x1, r2, ALU.subtract))
        vec.tensor_tensor(x2, x2, r1, ALU.add).then_inc(S("qk_ready"), 1)
        dve.wait_ge(S("qk_ready"), 1)
        for t in range(BLOCKS):
            kh = qkv[:, t, 1024:1152].rearrange("p (h e) -> p h e", e=HD)
            for i in range(2):
                ins = vec.tensor_copy(kd[:, t, :].rearrange("p (h i e) -> p h i e", h=KV, i=2)[:, :, i, :], kh)
        ins.then_inc(S("kd_ready"), 1)

        for p in range(8):
            g = p // 2
            dve.wait_ge(S("pool_copied"), p + 1)
            if p >= 1:
                dve.wait_ge(S("pl_ready"), p)
            u = pw[:, p % 2, :]
            cur = u
            for i in range(g + 1):
                d, nxt = 1 << i, pw[:, 2 + i % 2, :]
                order.done(vec.tensor_copy(nxt[:, 0:d], cur[:, 0:d]))
                link(vec.tensor_tensor(nxt[:, d:], cur[:, d:], cur[:, :T - d], ALU.add))
                cur = nxt
            res = pw[:, 2 + (g + 1) % 2, :]
            order.done(vec.scalar_tensor_tensor(res[:, 16:], cur[:, 16:], 1.0 / POOL_WINDOWS[g], u[:, 16:], ALU.mult, ALU.subtract))
            c0 = CONST["inv_count"] + 16 * g
            link(vec.tensor_tensor(res[:, 0:16], cur[:, 0:16], cst[:, c0:c0 + 16], ALU.mult))
            vec.tensor_tensor(res[:, 0:16], res[:, 0:16], u[:, 0:16], ALU.subtract).then_inc(S("pooled"), 1)
            dve.wait_ge(S("pl_hi_ready"), p + 1)
            vec.tensor_tensor(pl_lo[:, p, :], res, pl_hi[:, p, :].bitcast(F32), ALU.subtract).then_inc(S("pl_ready"), 1)
        for i in range(2):
            for n in range(4):
                if n < 3:
                    dve.wait_ge(S("mixed"), 3 * i + n + 1)
                else:
                    dve.wait_ge(S("units_done"), FIRST["wpool"] + i + 1)
                p = 4 * i + n
                vec.tensor_scalar(ya[:, p, :], ps[:, 4 + n, :], column("pool_scale_2", p), 0.5, ALU.mult, ALU.mult)\
                    .then_inc(S("ya_ready"), 1)

        STEPS = 4 * BLOCKS

        def maxima(s):
            n, g = s // 4, s % 4
            keys = slice(0 if n else P, 2 * P)
            stat = att_stat[:, n % 2]
            dve.wait_ge(S("scores_mm"), s + 1)
            if s >= 2:
                dve.wait_ge(S("probs_turned"), 2 * s - 2)
            for i in range(4):
                h = 4 * g + i
                at = (i // 2) * 256
                vec.tensor_tensor_reduce(scores_sb[:, (s % 2) * 4 + i, keys], ps[:, 2 + i % 2, at + keys.start:at + 256],
                                         cst[:, CONST["band"] + keys.start:CONST["band"] + 256], 1.0, sinks[:, h:h + 1],
                                         ALU.add, ALU.max, stat[:, 0, h:h + 1]).then_inc(S("scores_taken"), 1)
            dve.wait_ge(S("scores_taken"), 4 * s + 4)
            hs = slice(4 * g, 4 * g + 4)
            vec.tensor_scalar(stat[:, 1, hs], stat[:, 0, hs], -1.0, None, ALU.mult).then_inc(S("max_negated"), 1)
            if g == 3:
                dve.wait_ge(S("max_negated"), s + 1)
                vec.tensor_tensor(stat[:, 3, :], sinks[:, :], stat[:, 1, :], ALU.add).then_inc(S("sink_offset"), 1)

        def outputs(n):
            stat = att_stat[:, n % 2]
            dve.wait_ge(S("probs_ready"), 16 * n + 16)
            dve.wait_ge(S("sink_part"), n + 1)
            link(vec.tensor_tensor(stat[:, 2, :], stat[:, 2, :], stat[:, 3, :], ALU.add))
            link(vec.reciprocal(stat[:, 4, :], stat[:, 2, :]))
            if n >= 1:
                dve.wait_ge(S("o_turned"), 2 * n)
            for i in range(2):
                dve.wait_ge(S("weighed"), 4 * n + 2 * i + 2)
                vec.scalar_tensor_tensor(o_tok[:, i, :].rearrange("p (h e) -> p h e", e=HD),
                                         ps[:, 6 + i, :].rearrange("p (h e) -> p h e", e=HD), 0.5,
                                         stat[:, 4, 8 * i:8 * i + 8].unsqueeze(2).broadcast_to([P, 8, HD]),
                                         ALU.mult, ALU.mult).then_inc(S("o_tok_ready"), 1)

        def pool_gated(k):
            dve.wait_ge(S("gate_tanh"), k + 1)
            vec.scalar_tensor_tensor(ya[:, k, :], ga[:, k, :], 1.0, ya[:, k, :], ALU.add, ALU.mult).then_inc(S("pool_gated"), 1)

        def attention_gated(k, tok):
            link(vec.scalar_tensor_tensor(qT[:, k, tok], ga[:, k, tok], 1.0, qT[:, k, tok], ALU.add, ALU.mult))
            return vec.tensor_tensor(qT[:, k, tok], qT[:, k, tok], ya[:, k, tok], ALU.add)

        maxima(0)
        for s in range(STEPS):
            if s and s % 4 == 0:
                outputs(s // 4 - 1)
            if s + 1 < STEPS:
                maxima(s + 1)
            if s == 0:
                for k in range(EARLY):
                    pool_gated(k)
            elif gate_done_in(s - 1) in (6, 7):
                pool_gated(gate_done_in(s - 1))
            if s >= STEPS - 3:
                if s == STEPS - 3:
                    dve.wait_ge(S("pool_gated"), 8)
                    dve.wait_ge(S("bT_copied"), 2 * BLOCKS - 2)
                for k in ((0, 1, 2, 3), (4, 5), (6,))[s - STEPS + 3]:
                    dve.wait_ge(S("gate_tanh"), 9 + k)
                    order.done(attention_gated(k, slice(0, T - P)))
        outputs(BLOCKS - 1)
        dve.wait_ge(S("gate_tanh"), 16)
        order.done(attention_gated(KT - 1, slice(0, T - P)))
        for half in range(2):
            dve.wait_ge(S("bT_copied"), 2 * BLOCKS - 1 + half)
            attention_gated(slice(4 * half, 4 * half + 4), slice(T - P, T)).then_inc(S("y2_sum"), 1)
        for k in range(KT):
            dve.wait_ge(S("y2_hi_ready"), k + 1)
            vec.tensor_tensor(y2_lo[:, k, :], qT[:, k, :], y2_hi[:, k, :].bitcast(F32), ALU.subtract).then_inc(S("y2_ready"), 1)

        for m in range(KT):
            dve.wait_ge(S("units_done"), FIRST["out2"] + m + 1)
            vec.tensor_tensor(xT[:, m, :], xT[:, m, :], ps[:, (m + 7) % 8, :], ALU.add).then_inc(S("x_ready"), 1)
        invert(6)
        modulated(6, 4, lambda m: xT[:, m, :], lambda m: column("ffn_norm_2", m), lambda m: const("zero"), h_hi, h_lo)
        ffn(1, "up2")
        for m in range(KT):
            if m < KT - 1:
                dve.wait_ge(S("down_done"), 7 + m + 1)
            else:
                dve.wait_ge(S("units_done"), UNITS)
            vec.tensor_tensor(xT[:, m, :], xT[:, m, :], ps[:, (m + 7) % 8, :], ALU.add).then_inc(S("final_ready"), 1)

    ctx.close()


MATRICES = {"x": (T, D), "ctx": (TC, D), "w_ada": (D, 6 * D), "w_in": (D, -1), "w_af": (16, -1), "w_ab": (16, -1),
            "w_out": (D, D), "w_up": (D, -1), "w_down": (FF, D), "w_in_2": (D, -1), "w_pool_2": (D, 256),
            "w_out_2": (D, D), "w_up_2": (D, -1), "w_down_2": (FF, D)}
VECTORS = ["c", "c_ctx", "b_ada", "g_pre_mix", "g_post_mix", "g_pre_ffn", "g_post_ffn", "b_af", "b_ab", "g_head", "w_sc",
           "b_sc", "w_cf", "b_cf", "positions_2", "attn_norm_2", "b_gate_2", "pool_scale_2", "q_norm_2", "k_norm_2",
           "sinks_2", "ffn_norm_2", "conv_w_2", "conv_b_2"]


def kernel(**inputs):
    import concourse.bacc as bacc
    from concourse.bass_utils import run_bass_kernel_spmd

    nc = bacc.Bacc("TRN2", target_bir_lowering=False, num_devices=1)
    arrays = {name: np.ascontiguousarray(inputs[name]).reshape(shape) for name, shape in MATRICES.items()}
    arrays |= {name: np.ascontiguousarray(inputs[name]).reshape(-1) for name in VECTORS}
    arrays |= {"consts": shape_constants(), "masks": shape_masks()}
    aps = {name: nc.dram_tensor(f"in_{name}", x.shape, mybir.dt.from_np(x.dtype), kind="ExternalInput").ap()
           for name, x in arrays.items()}
    out = nc.dram_tensor("out", (T, D), F32, kind="ExternalOutput").ap()
    build_program(nc, aps, out)
    result = run_bass_kernel_spmd(nc, [{f"in_{name}": x for name, x in arrays.items()}], core_ids=[0])
    return result.results[0]["out"].reshape(1, T, D)
```
